# Optimizing a Trainium2 kernel written in Bass

```python
import math
import jax, jax.numpy as jnp
from jax import lax
import numpy as np

D_MODEL = 1024
BATCH = 1
SEQ = 512
DEPTH = 1

N_MEM = 256
MIX_WIDTH = D_MODEL
DA_WIDTH = MIX_WIDTH // 2
CV_WIDTH = MIX_WIDTH - DA_WIDTH
DA_HEADS = 4
DA_VDIM = DA_WIDTH // DA_HEADS
DA_QKDIM = DA_VDIM // 2
ROT_DIM = DA_QKDIM // 4
ROPE_THETA = 500000.0
Q_BLOCK = 128
CV_KERNEL = 31
X_HEADS = 4
X_HEAD_DIM = D_MODEL // X_HEADS
D_FF = 2816
FFN_KERNEL = 3
EPS = 1e-6

Q_COLS = DA_HEADS * 2 * DA_QKDIM
K_COLS = DA_HEADS * 2 * DA_QKDIM
V_COLS = DA_HEADS * DA_VDIM
CV_COLS = 2 * CV_WIDTH
IN_COLS = Q_COLS + K_COLS + V_COLS + CV_COLS


def rmsnorm(x, g):
    xf = x.astype(jnp.float32)
    y = xf * lax.rsqrt(jnp.mean(xf * xf, axis=-1, keepdims=True) + EPS)
    return (y * g.astype(jnp.float32)).astype(x.dtype)

def layernorm(x, g, b):
    xf = x.astype(jnp.float32)
    mu = jnp.mean(xf, axis=-1, keepdims=True)
    var = jnp.mean(jnp.square(xf - mu), axis=-1, keepdims=True)
    y = (xf - mu) * lax.rsqrt(var + EPS)
    return (y * g.astype(jnp.float32) + b.astype(jnp.float32)).astype(x.dtype)

def causal_dwconv(x, w):
    k, c = w.shape
    return lax.conv_general_dilated(
        x, w[:, None, :].astype(x.dtype), window_strides=(1,),
        padding=[(k - 1, 0)], dimension_numbers=("NWC", "WIO", "NWC"),
        feature_group_count=c)

def partial_rope(t, positions):
    half = ROT_DIM // 2
    inv_freq = ROPE_THETA ** (-jnp.arange(0, ROT_DIM, 2, dtype=jnp.float32) / ROT_DIM)
    ang = positions.astype(jnp.float32)[..., None] * inv_freq
    cos = jnp.cos(ang)[:, :, None, None, :]
    sin = jnp.sin(ang)[:, :, None, None, :]
    tf = t.astype(jnp.float32)
    t1, t2, rest = tf[..., :half], tf[..., half:ROT_DIM], tf[..., ROT_DIM:]
    out = jnp.concatenate([t1 * cos - t2 * sin, t2 * cos + t1 * sin, rest], axis=-1)
    return out.astype(t.dtype)

def diff_attention(q, k, v, lam):
    b, h, _, s, d = q.shape
    dv = v.shape[-1]
    nblk = s // Q_BLOCK
    scale = 1.0 / math.sqrt(d)
    qb = q.reshape(b, h, 2, nblk, Q_BLOCK, d).transpose(3, 0, 1, 2, 4, 5)
    kpos = jnp.arange(s)

    def one_block(args):
        q_blk, i = args
        sc = jnp.einsum("bhcqd,bhckd->bhcqk", q_blk, k).astype(jnp.float32) * scale
        qpos = i * Q_BLOCK + jnp.arange(Q_BLOCK)
        mask = kpos[None, :] <= qpos[:, None]
        sc = jnp.where(mask, sc, -jnp.inf)
        p = jax.nn.softmax(sc, axis=-1)
        a = p[:, :, 0] - lam * p[:, :, 1]
        return jnp.einsum("bhqk,bhkv->bhqv", a.astype(v.dtype), v)

    out = lax.map(one_block, (qb, jnp.arange(nblk)))
    return out.transpose(1, 0, 3, 2, 4).reshape(b, s, h, dv)

def hybrid_mixer(h, positions, layer_idx, w_in, lam_q1, lam_k1, lam_q2, lam_k2,
                 subln_g, cv_dw_w, cv_dw_b, cv_ln_g, cv_ln_b, w_out):
    b, s, _ = h.shape
    proj = jnp.einsum("bsd,dc->bsc", h, w_in)
    o1 = Q_COLS
    o2 = o1 + K_COLS
    o3 = o2 + V_COLS
    q = proj[..., :o1].reshape(b, s, DA_HEADS, 2, DA_QKDIM)
    k = proj[..., o1:o2].reshape(b, s, DA_HEADS, 2, DA_QKDIM)
    v = proj[..., o2:o3].reshape(b, s, DA_HEADS, DA_VDIM)
    u = proj[..., o3:]

    q = partial_rope(q, positions).transpose(0, 2, 3, 1, 4)
    k = partial_rope(k, positions).transpose(0, 2, 3, 1, 4)
    v = v.transpose(0, 2, 1, 3)
    lam_init = 0.8 - 0.6 * math.exp(-0.3 * layer_idx)
    lam = (jnp.exp(jnp.sum(lam_q1.astype(jnp.float32) * lam_k1.astype(jnp.float32)))
           - jnp.exp(jnp.sum(lam_q2.astype(jnp.float32) * lam_k2.astype(jnp.float32)))
           + lam_init)
    a = diff_attention(q, k, v, lam)
    a = rmsnorm(a, subln_g) * (1.0 - lam_init)
    a = a.reshape(b, s, DA_WIDTH)

    c = u[..., :CV_WIDTH] * jax.nn.sigmoid(u[..., CV_WIDTH:])
    c = causal_dwconv(c, cv_dw_w) + cv_dw_b.astype(c.dtype)
    c = jax.nn.silu(layernorm(c, cv_ln_g, cv_ln_b))

    y = jnp.concatenate([a, c], axis=-1)
    return jnp.einsum("bsc,cd->bsd", y, w_out)

def cross_attention(h, m, w_cq, w_ckv, w_co):
    b, s, _ = h.shape
    q = jnp.einsum("bsd,de->bse", h, w_cq).reshape(b, s, X_HEADS, X_HEAD_DIM)
    kv = jnp.einsum("bmd,de->bme", m, w_ckv)
    k = kv[..., :D_MODEL].reshape(b, m.shape[1], X_HEADS, X_HEAD_DIM)
    v = kv[..., D_MODEL:].reshape(b, m.shape[1], X_HEADS, X_HEAD_DIM)
    sc = jnp.einsum("bshd,bmhd->bhsm", q, k).astype(jnp.float32) / math.sqrt(X_HEAD_DIM)
    p = jax.nn.softmax(sc, axis=-1).astype(v.dtype)
    o = jnp.einsum("bhsm,bmhd->bshd", p, v).reshape(b, s, D_MODEL)
    return jnp.einsum("bse,ed->bsd", o, w_co)

def conv_ffn(h, w_up, ffn_dw_w, w_down):
    up = jnp.einsum("bsd,df->bsf", h, w_up)
    up = causal_dwconv(up, ffn_dw_w)
    z = jax.nn.silu(up[..., :D_FF]) * up[..., D_FF:]
    return jnp.einsum("bsf,fd->bsd", z, w_down)

def first_inputs(seed: int = 0) -> dict:
    key = jax.random.key(seed)
    ks = jax.random.split(key, 24)
    f32 = jnp.float32

    def nrm(k, shape, scale):
        return jax.random.normal(k, shape, f32) * scale

    def gain(k, shape):
        return 1.0 + 0.02 * jax.random.normal(k, shape, f32)

    L = DEPTH
    return {
        "x": jax.random.normal(ks[0], (BATCH, SEQ, D_MODEL), f32),
        "mem": jax.random.normal(ks[1], (BATCH, N_MEM, D_MODEL), f32),
        "positions": jnp.broadcast_to(jnp.arange(SEQ, dtype=jnp.int32), (BATCH, SEQ)),
        "norm_mix_g": gain(ks[2], (L, D_MODEL)),
        "w_in": nrm(ks[3], (L, D_MODEL, IN_COLS), D_MODEL ** -0.5),
        "lam_q1": nrm(ks[4], (L, DA_QKDIM), 0.1),
        "lam_k1": nrm(ks[5], (L, DA_QKDIM), 0.1),
        "lam_q2": nrm(ks[6], (L, DA_QKDIM), 0.1),
        "lam_k2": nrm(ks[7], (L, DA_QKDIM), 0.1),
        "subln_g": gain(ks[8], (L, DA_VDIM)),
        "cv_dw_w": nrm(ks[9], (L, CV_KERNEL, CV_WIDTH), CV_KERNEL ** -0.5),
        "cv_dw_b": nrm(ks[10], (L, CV_WIDTH), 0.02),
        "cv_ln_g": gain(ks[11], (L, CV_WIDTH)),
        "cv_ln_b": nrm(ks[12], (L, CV_WIDTH), 0.02),
        "w_out": nrm(ks[13], (L, MIX_WIDTH, D_MODEL), MIX_WIDTH ** -0.5),
        "norm_cross_g": gain(ks[14], (L, D_MODEL)),
        "norm_mem_g": gain(ks[15], (L, D_MODEL)),
        "w_cq": nrm(ks[16], (L, D_MODEL, D_MODEL), D_MODEL ** -0.5),
        "w_ckv": nrm(ks[17], (L, D_MODEL, 2 * D_MODEL), D_MODEL ** -0.5),
        "w_co": nrm(ks[18], (L, D_MODEL, D_MODEL), D_MODEL ** -0.5),
        "norm_ffn_g": gain(ks[19], (L, D_MODEL)),
        "w_up": nrm(ks[20], (L, D_MODEL, 2 * D_FF), D_MODEL ** -0.5),
        "ffn_dw_w": nrm(ks[21], (L, FFN_KERNEL, 2 * D_FF), FFN_KERNEL ** -0.5),
        "w_down": nrm(ks[22], (L, D_FF, D_MODEL), D_FF ** -0.5),
        "norm_final_g": gain(ks[23], (D_MODEL,)),
    }

def first_block(x, mem, positions, norm_mix_g, w_in, lam_q1, lam_k1, lam_q2, lam_k2,
              subln_g, cv_dw_w, cv_dw_b, cv_ln_g, cv_ln_b, w_out,
              norm_cross_g, norm_mem_g, w_cq, w_ckv, w_co,
              norm_ffn_g, w_up, ffn_dw_w, w_down, norm_final_g):
    h = x
    for l in range(DEPTH):
        h = h + hybrid_mixer(rmsnorm(h, norm_mix_g[l]), positions, l, w_in[l],
                             lam_q1[l], lam_k1[l], lam_q2[l], lam_k2[l], subln_g[l],
                             cv_dw_w[l], cv_dw_b[l], cv_ln_g[l], cv_ln_b[l], w_out[l])
        h = h + cross_attention(rmsnorm(h, norm_cross_g[l]), rmsnorm(mem, norm_mem_g[l]),
                                w_cq[l], w_ckv[l], w_co[l])
        h = h + conv_ffn(rmsnorm(h, norm_ffn_g[l]), w_up[l], ffn_dw_w[l], w_down[l])
    return rmsnorm(h, norm_final_g)


SB_HEADS = 8
SB_HEAD_DIM = 128
SB_WIDTH = SB_HEADS * SB_HEAD_DIM
SB_BLOCK = 128
GDN_HEADS = 8
GDN_HEAD_DIM = 128
GDN_WIDTH = GDN_HEADS * GDN_HEAD_DIM
GDN_CONV = 4
GDN_CHUNK = 64
PEER_HEADS = 8
PEER_N_KEYS = 128
PEER_N_EXPERTS = PEER_N_KEYS * PEER_N_KEYS
PEER_D_KEY = 256
PEER_HALF = PEER_D_KEY // 2
PEER_TOPK = 16
PEER_TOKEN_BLOCK = 128
IN_WIDTH = 3 * SB_WIDTH + 3 * GDN_WIDTH + GDN_WIDTH + 2 * GDN_HEADS + 2 * D_MODEL


def rms_norm(x, w):
    xf = x.astype(jnp.float32)
    y = xf * lax.rsqrt(jnp.mean(xf * xf, axis=-1, keepdims=True) + EPS)
    return (y * w.astype(jnp.float32)).astype(x.dtype)

def l2_normalize(x):
    xf = x.astype(jnp.float32)
    return xf * lax.rsqrt(jnp.sum(xf * xf, axis=-1, keepdims=True) + EPS)

def stick_breaking_attention(q, k, v):
    S, Dh = q.shape[2], q.shape[3]
    scale = Dh ** -0.5
    qf, kf, vf = q.astype(jnp.float32), k.astype(jnp.float32), v.astype(jnp.float32)
    outs = []
    for blk in range(S // SB_BLOCK):
        t0 = blk * SB_BLOCK
        t1 = t0 + SB_BLOCK
        z = jnp.einsum('bhqd,bhkd->bhqk', qf[:, :, t0:t1], kf[:, :, :t1]) * scale
        t_idx = t0 + jnp.arange(SB_BLOCK)[:, None]
        s_idx = jnp.arange(t1)[None, :]
        causal = s_idx < t_idx
        log_1mb = jnp.where(causal, jax.nn.log_sigmoid(-z), 0.0)
        suffix = lax.cumsum(log_1mb, axis=3, reverse=True) - log_1mb
        log_a = jax.nn.log_sigmoid(z) + suffix
        a = jnp.where(causal, jnp.exp(log_a), 0.0)
        outs.append(jnp.einsum('bhqk,bhkd->bhqd', a, vf[:, :, :t1]))
    return jnp.concatenate(outs, axis=2).astype(q.dtype)

def causal_depthwise_conv(x, w):
    K = w.shape[0]
    S = x.shape[1]
    xp = jnp.pad(x, ((0, 0), (K - 1, 0), (0, 0)))
    return sum(xp[:, i:i + S] * w[i] for i in range(K))

def gated_delta_rule_chunked(q, k, v, g, beta):
    B, H, S, Dk = q.shape
    Dv = v.shape[-1]
    C = GDN_CHUNK
    n = S // C
    q = q * (Dk ** -0.5)
    qc = q.reshape(B, H, n, C, Dk)
    kc = k.reshape(B, H, n, C, Dk)
    vc = v.reshape(B, H, n, C, Dv)
    gc = jnp.cumsum(g.reshape(B, H, n, C), axis=-1)
    bc = beta.reshape(B, H, n, C)
    k_beta = kc * bc[..., None]
    v_beta = vc * bc[..., None]
    tril = jnp.tril(jnp.ones((C, C), dtype=bool))
    strict = jnp.tril(jnp.ones((C, C), dtype=bool), -1)
    gdiff = gc[..., :, None] - gc[..., None, :]
    decay = jnp.where(tril, jnp.exp(jnp.where(tril, gdiff, 0.0)), 0.0)
    L = jnp.where(strict, jnp.einsum('bhnid,bhnjd->bhnij', k_beta, kc) * decay, 0.0)
    eye = jnp.eye(C, dtype=L.dtype)
    T = lax.linalg.triangular_solve(eye + L, jnp.broadcast_to(eye, L.shape),
                                    left_side=True, lower=True, unit_diagonal=True)
    v_corr = jnp.einsum('bhnij,bhnjd->bhnid', T, v_beta)
    k_cumdecay = jnp.einsum('bhnij,bhnjd->bhnid', T, k_beta * jnp.exp(gc)[..., None])
    attn_intra = jnp.where(tril, jnp.einsum('bhnid,bhnjd->bhnij', qc, kc) * decay, 0.0)

    def step(state, inp):
        q_i, k_i, v_i, kcd_i, g_i, a_i = inp
        v_new = v_i - jnp.einsum('bhcd,bhde->bhce', kcd_i, state)
        o = (jnp.einsum('bhcd,bhde->bhce', q_i * jnp.exp(g_i)[..., None], state)
             + jnp.einsum('bhij,bhje->bhie', a_i, v_new))
        g_last = g_i[..., -1]
        k_w = k_i * jnp.exp(g_last[..., None] - g_i)[..., None]
        state = state * jnp.exp(g_last)[..., None, None] + jnp.einsum('bhcd,bhce->bhde', k_w, v_new)
        return state, o

    to_front = lambda t: jnp.moveaxis(t, 2, 0)
    xs = (to_front(qc), to_front(kc), to_front(v_corr), to_front(k_cumdecay), to_front(gc), to_front(attn_intra))
    state0 = jnp.zeros((B, H, Dk, Dv), dtype=jnp.float32)
    _, o = lax.scan(step, state0, xs)
    return jnp.moveaxis(o, 0, 2).reshape(B, H, S, Dv)

def peer_ffn(h, w_q, keys1, keys2, u_tab, v_tab):
    B, S, D = h.shape
    q = jnp.einsum('bsd,de->bse', h, w_q).astype(jnp.float32).reshape(B, S, PEER_HEADS, PEER_D_KEY)
    s1 = jnp.einsum('bshd,hnd->bshn', q[..., :PEER_HALF], keys1.astype(jnp.float32))
    s2 = jnp.einsum('bshd,hnd->bshn', q[..., PEER_HALF:], keys2.astype(jnp.float32))
    v1, i1 = lax.top_k(s1, PEER_TOPK)
    v2, i2 = lax.top_k(s2, PEER_TOPK)
    cand = (v1[..., :, None] + v2[..., None, :]).reshape(B, S, PEER_HEADS, PEER_TOPK * PEER_TOPK)
    vals, c = lax.top_k(cand, PEER_TOPK)
    e1 = jnp.take_along_axis(i1, c // PEER_TOPK, axis=-1)
    e2 = jnp.take_along_axis(i2, c % PEER_TOPK, axis=-1)
    expert = e1 * PEER_N_KEYS + e2
    gate = jax.nn.softmax(vals, axis=-1)
    n_tok = B * S
    nb = n_tok // PEER_TOKEN_BLOCK
    hk = PEER_HEADS * PEER_TOPK
    hx = h.reshape(nb, PEER_TOKEN_BLOCK, D)
    ex = expert.reshape(nb, PEER_TOKEN_BLOCK, hk)
    gx = gate.reshape(nb, PEER_TOKEN_BLOCK, hk).astype(h.dtype)

    def block(args):
        hb, eb, gb = args
        u = u_tab[eb]
        act = jax.nn.gelu(jnp.einsum('td,ted->te', hb, u), approximate=False)
        v = v_tab[eb]
        return jnp.einsum('te,ted->td', gb * act, v)

    out = lax.map(block, (hx, ex, gx))
    return out.reshape(B, S, D).astype(h.dtype)

def second_inputs(seed: int = 0) -> dict:
    key = jax.random.key(seed)
    ks = jax.random.split(key, 20)
    f32 = jnp.float32
    nrm = lambda k, shape, scale: jax.random.normal(k, shape, f32) * scale
    gain = lambda k, shape: 1.0 + 0.02 * jax.random.normal(k, shape, f32)
    dt = jnp.exp(jax.random.uniform(ks[7], (DEPTH, GDN_HEADS), f32, np.log(1e-3), np.log(1e-1)))
    return {
        "x": jax.random.normal(ks[0], (BATCH, SEQ, D_MODEL), f32),
        "mix_norm_w": gain(ks[1], (DEPTH, D_MODEL)),
        "w_in": nrm(ks[2], (DEPTH, D_MODEL, IN_WIDTH), D_MODEL ** -0.5),
        "sb_q_norm_w": gain(ks[3], (DEPTH, SB_HEAD_DIM)),
        "sb_k_norm_w": gain(ks[4], (DEPTH, SB_HEAD_DIM)),
        "gdn_conv_w": nrm(ks[5], (DEPTH, GDN_CONV, 3 * GDN_WIDTH), GDN_CONV ** -0.5),
        "gdn_a_log": jnp.log(jax.random.uniform(ks[6], (DEPTH, GDN_HEADS), f32, 1.0, 16.0)),
        "gdn_dt_bias": dt + jnp.log(-jnp.expm1(-dt)),
        "gdn_out_norm_w": gain(ks[8], (DEPTH, GDN_HEAD_DIM)),
        "w_branch_sb": nrm(ks[9], (DEPTH, SB_WIDTH, D_MODEL), SB_WIDTH ** -0.5),
        "w_branch_gdn": nrm(ks[10], (DEPTH, GDN_WIDTH, D_MODEL), GDN_WIDTH ** -0.5),
        "w_out": nrm(ks[11], (DEPTH, D_MODEL, D_MODEL), D_MODEL ** -0.5),
        "ffn_norm_w": gain(ks[12], (DEPTH, D_MODEL)),
        "peer_w_q": nrm(ks[13], (DEPTH, D_MODEL, PEER_HEADS * PEER_D_KEY), D_MODEL ** -0.5),
        "peer_keys1": nrm(ks[14], (DEPTH, PEER_HEADS, PEER_N_KEYS, PEER_HALF), PEER_HALF ** -0.5),
        "peer_keys2": nrm(ks[15], (DEPTH, PEER_HEADS, PEER_N_KEYS, PEER_HALF), PEER_HALF ** -0.5),
        "peer_u": nrm(ks[16], (DEPTH, PEER_N_EXPERTS, D_MODEL), D_MODEL ** -0.5),
        "peer_v": nrm(ks[17], (DEPTH, PEER_N_EXPERTS, D_MODEL), PEER_TOPK ** -0.5),
    }

def second_block(x, mix_norm_w, w_in, sb_q_norm_w, sb_k_norm_w, gdn_conv_w, gdn_a_log, gdn_dt_bias,
              gdn_out_norm_w, w_branch_sb, w_branch_gdn, w_out, ffn_norm_w, peer_w_q, peer_keys1,
              peer_keys2, peer_u, peer_v):
    B, S, D = x.shape
    f32 = jnp.float32
    sizes = [3 * SB_WIDTH, 3 * GDN_WIDTH, GDN_WIDTH, GDN_HEADS, GDN_HEADS, D_MODEL, D_MODEL]
    offsets = np.cumsum(sizes)[:-1].tolist()
    for l in range(DEPTH):
        h = rms_norm(x, mix_norm_w[l])
        proj = jnp.einsum('bsd,de->bse', h, w_in[l])
        sb_qkv, gdn_qkv, gdn_z, gdn_b, gdn_a, gate_sb, gate_gdn = jnp.split(proj, offsets, axis=-1)

        heads_sb = lambda t: t.reshape(B, S, SB_HEADS, SB_HEAD_DIM).transpose(0, 2, 1, 3)
        q, k, v = [heads_sb(t) for t in jnp.split(sb_qkv, 3, axis=-1)]
        q = rms_norm(q, sb_q_norm_w[l])
        k = rms_norm(k, sb_k_norm_w[l])
        o_sb = stick_breaking_attention(q, k, v).transpose(0, 2, 1, 3).reshape(B, S, SB_WIDTH)

        qkv = jax.nn.silu(causal_depthwise_conv(gdn_qkv, gdn_conv_w[l]))
        heads_gdn = lambda t: t.reshape(B, S, GDN_HEADS, GDN_HEAD_DIM).transpose(0, 2, 1, 3)
        gq, gk, gv = [heads_gdn(t) for t in jnp.split(qkv, 3, axis=-1)]
        gq = l2_normalize(gq)
        gk = l2_normalize(gk)
        gv = gv.astype(f32)
        beta = jax.nn.sigmoid(gdn_b.astype(f32)).transpose(0, 2, 1)
        g = -(jnp.exp(gdn_a_log[l].astype(f32))
              * jax.nn.softplus(gdn_a.astype(f32) + gdn_dt_bias[l].astype(f32))).transpose(0, 2, 1)
        o_gdn = gated_delta_rule_chunked(gq, gk, gv, g, beta).transpose(0, 2, 1, 3)
        z = gdn_z.reshape(B, S, GDN_HEADS, GDN_HEAD_DIM).astype(f32)
        o_gdn = (rms_norm(o_gdn, gdn_out_norm_w[l]) * jax.nn.silu(z)).reshape(B, S, GDN_WIDTH).astype(x.dtype)

        y_sb = jnp.einsum('bse,ed->bsd', o_sb, w_branch_sb[l])
        y_gdn = jnp.einsum('bse,ed->bsd', o_gdn, w_branch_gdn[l])
        merged = jax.nn.sigmoid(gate_sb) * y_sb + jax.nn.sigmoid(gate_gdn) * y_gdn
        x = x + jnp.einsum('bsd,de->bse', merged, w_out[l])

        h2 = rms_norm(x, ffn_norm_w[l])
        x = x + peer_ffn(h2, peer_w_q[l], peer_keys1[l], peer_keys2[l], peer_u[l], peer_v[l])
    return x


def setup_inputs(seed=0):
    out = dict(first_inputs(seed))
    for name, value in second_inputs(seed + 1).items():
        if name != "x":
            out[name + "_2"] = value
    return out


def reference(
    x, mem, positions, norm_mix_g, w_in, lam_q1, lam_k1, lam_q2, lam_k2, subln_g, cv_dw_w,
    cv_dw_b, cv_ln_g, cv_ln_b, w_out, norm_cross_g, norm_mem_g, w_cq, w_ckv, w_co, norm_ffn_g,
    w_up, ffn_dw_w, w_down, norm_final_g, mix_norm_w_2, w_in_2, sb_q_norm_w_2, sb_k_norm_w_2,
    gdn_conv_w_2, gdn_a_log_2, gdn_dt_bias_2, gdn_out_norm_w_2, w_branch_sb_2, w_branch_gdn_2,
    w_out_2, ffn_norm_w_2, peer_w_q_2, peer_keys1_2, peer_keys2_2, peer_u_2, peer_v_2,
):
    x = first_block(
        x, mem, positions, norm_mix_g, w_in, lam_q1, lam_k1, lam_q2, lam_k2, subln_g, cv_dw_w,
        cv_dw_b, cv_ln_g, cv_ln_b, w_out, norm_cross_g, norm_mem_g, w_cq, w_ckv, w_co,
        norm_ffn_g, w_up, ffn_dw_w, w_down, norm_final_g,
    )
    return second_block(
        x, mix_norm_w_2, w_in_2, sb_q_norm_w_2, sb_k_norm_w_2, gdn_conv_w_2, gdn_a_log_2,
        gdn_dt_bias_2, gdn_out_norm_w_2, w_branch_sb_2, w_branch_gdn_2, w_out_2, ffn_norm_w_2,
        peer_w_q_2, peer_keys1_2, peer_keys2_2, peer_u_2, peer_v_2,
    )


_drawn_inputs = setup_inputs


def setup_inputs(seed=0):
    import zlib

    import numpy as np

    out = dict(_drawn_inputs(seed))
    spreads = {}
    factors = {'subln_g': 3.09,
     'cv_ln_g': 3.518,
     'cv_ln_b': 3.933,
     'norm_cross_g': 8.0,
     'norm_mem_g': 7.666,
     'norm_ffn_g': 2.794,
     'mix_norm_w_2': 2.962,
     'sb_q_norm_w_2': 25.807,
     'sb_k_norm_w_2': 25.842,
     'gdn_out_norm_w_2': 15.914,
     'ffn_norm_w_2': 26.24}
    for name, (base, spread) in spreads.items():
        noise = np.random.default_rng([zlib.crc32(name.encode()), seed]).standard_normal(out[name].shape)
        drawn = base * np.exp(spread * noise) if base else spread * noise
        out[name] = __import__('jax').numpy.asarray(drawn.astype(out[name].dtype))
    for name, factor in factors.items():
        out[name] = (out[name] * factor).astype(out[name].dtype)
    return out
```

```python
import math
from contextlib import ExitStack

import numpy as np

import concourse.bass as bass
from concourse import mybir

P = 128
F32 = mybir.dt.float32
F32R = mybir.dt.float32r
U32 = mybir.dt.uint32
I32 = mybir.dt.int32
ALU = mybir.AluOpType
ACT = mybir.ActivationFunctionType
AX = mybir.AxisListType.X

D = 1024
S = 512
KB = D // P
TB = S // P
NMEM = 256
MB = NMEM // P
EPS = 1e-6
TAPS = 31
FFB = 2816 // P
NH2 = 8
GROUPS = 16
TG = S // 32
NEG = -1e30

CONSTS = {}
_at = 0
for _name, _n in (("ident", P), ("ones", P), ("swap", P), ("causal", P), ("low", P), ("ups", P), ("upi", P),
                  ("levels", 7 * P), ("iota", P), ("invfreq", 1)):
    CONSTS[_name] = (_at, _n)
    _at += _n
N_CONST = _at

PARAMS = {}
_at = 0
for _name, _n in (("norm_mix", 8), ("norm_cross", 8), ("norm_mem", 8), ("norm_ffn", 8), ("norm_final", 8),
                  ("mix2", 8), ("ffn2", 8), ("subln", 1), ("cv_w", 4 * TAPS), ("cv_b", 4), ("ln_g", 4),
                  ("ln_b", 4), ("ffn_w", 44 * 3), ("sbq", 1), ("sbk", 1), ("gdn_w", 24 * 4), ("gdn_g", 1),
                  ("lam", 4 * 64), ("a_log", 8), ("dt", 8)):
    PARAMS[_name] = (_at, _n)
    _at += _n
N_PARAM = _at

TILE = {}
_at = 0
for _name, _n in (("ckv", 16), ("in_u", 8), ("in_qkv", 12), ("out", 8), ("cq", 8), ("co", 8), ("up", 44),
                  ("down", 22), ("sb_qkv", 24), ("gate_sb", 8), ("branch_sb", 8), ("gdn_qkv", 24), ("ba", 1),
                  ("z", 8), ("gate_gdn", 8), ("branch_gdn", 8), ("out2", 8), ("wq", 16), ("peer", 16 * GROUPS)):
    TILE[_name] = _at
    _at += _n
N_TILES = _at


def constants():
    c = np.zeros((P, N_CONST), np.float32)
    r = np.arange(P)

    def put(name, a):
        o, n = CONSTS[name]
        c[:, o:o + n] = a

    put("ident", np.eye(P))
    put("ones", 1.0)
    swap = np.zeros((P, P))
    for half in range(2):
        for i in range(8):
            swap[64 * half + i + 8, 64 * half + i] = -1.0
            swap[64 * half + i, 64 * half + i + 8] = 1.0
    put("swap", swap)
    put("causal", np.where(r[None, :] <= r[:, None], 0.0, NEG))
    put("low", r[:, None] > r[None, :])
    put("ups", r[:, None] < r[None, :])
    put("upi", r[:, None] <= r[None, :])
    levels = np.zeros((P, 7, P))
    for n in range(7):
        b = 1 << n
        same = r[:, None] // (2 * b) == r[None, :] // (2 * b)
        levels[:, n, :] = same & (r[:, None] // b % 2 == 0) & (r[None, :] // b % 2 == 1)
    put("levels", levels.reshape(P, -1))
    put("iota", r[None, :])
    freq = np.float32(500000.0) ** (-np.arange(0, 16, 2, dtype=np.float32) / np.float32(16))
    col = np.zeros(P)
    for half in range(2):
        col[64 * half:64 * half + 8] = freq
        col[64 * half + 8:64 * half + 16] = freq
    put("invfreq", col[:, None])
    return c


class Chain:

    def __init__(self, eng, sem):
        self.eng, self.sem, self.n = eng, sem, 0

    def __call__(self, ins):
        ins.then_inc(self.sem, 1)
        self.n = self.n + 1
        self.eng.wait_ge(self.sem, self.n)


class Side:

    def __init__(self, eng, sems, barrier_name, others):
        self.eng, self.sems = eng, sems
        self.n = {}
        self.phase, self.me, self.others = 0, barrier_name, others

    def wait(self, name, k=1):
        self.n[name] = self.n.get(name, 0) + k
        self.eng.wait_ge(self.sems(name), self.n[name])

    def at(self, name, value):
        if value > 0:
            self.eng.wait_ge(self.sems(name), value)

    def made(self, name):
        k = self.n.get("made " + name, 0)
        self.n["made " + name] = k + 1
        return k

    def prime(self, name, k=1):
        self.eng.drain().then_inc(self.sems(name), k)

    def meet(self):
        self.phase += 1
        self.eng.drain().then_inc(self.sems(self.me), 1)
        for o in self.others:
            self.eng.wait_ge(self.sems(o), self.phase)


def build(nc, a, first=True, second=True):
    with ExitStack() as ctx:
        sem_of = {}

        def sems(name):
            if name not in sem_of:
                sem_of[name] = ctx.enter_context(nc.semaphore(name))
            return sem_of[name]

        def sb(name, shape, dt=F32, on=None):
            return (on or ctx).enter_context(nc.sbuf_tensor("sb_" + name, shape, dt))

        ps = [ctx.enter_context(nc.psum_tensor(f"bank{i}", [P, 512], F32)) for i in range(8)]

        cst = sb("consts", [P, N_CONST])
        par = sb("params", [P, N_PARAM])
        xT = sb("xT", [P, KB, S])
        hH = sb("hH", [P, KB, S], F32R)
        hL = sb("hL", [P, KB, S], F32R)
        raw = sb("raw", [P, 4, D])
        wH = sb("wH", [P, 2, D], F32R)
        wL = sb("wL", [P, 2, D], F32R)
        sq = sb("sq", [P, 4, S])
        tmp = sb("tmp", [P, 4, S])
        dg = sb("dg", [P, 2, S])
        st = sb("st", [P, 5, 64])

        def C(name, i=0, n=None):
            o, w = CONSTS[name]
            return cst[:, o + i:o + i + (n or w)]

        def PM(name, i=0, n=1):
            return par[:, PARAMS[name][0] + i:PARAMS[name][0] + i + n]

        ss = sb("ss", [P, 2, 16])
        cell = sb("cell", [P, 2])
        sc = sb("sc", [P, 16])

        def over(spec, inner=()):
            with ExitStack() as e:
                got = {n: sb(n, s, d, on=e) for n, s, d in spec}
                for more in inner:
                    got.update(more())
            return got

        B = {}
        B.update(over([("kmem", [P, 8, NMEM], F32), ("vmem", [P, MB, D], F32)], (
            lambda: over([("memT", [P, 8, NMEM], F32)]),
            lambda: over([("qkT", [P, 8, S], F32), ("vT", [P, 4, S], F32), ("vtok", [P, TB, S], F32),
                          ("cpad", [P, 4, S + 32], F32), ("cacc", [P, 4, S], F32), ("cos", [P, S], F32),
                          ("sin", [P, S], F32), ("pos", [P, S], I32), ("p", [P, 2, 2, S], F32),
                          ("att", [P, 2, S], F32), ("attT", [P, 2, S], F32), ("oT", [P, 4, S], F32)]),
            lambda: over([("qx", [P, 8, S], F32), ("px", [P, 2, NMEM], F32), ("pxT", [P, 2, MB, S], F32)]))))
        B.update(over([("zH", [P, FFB, S], F32R), ("zL", [P, FFB, S], F32R), ("uab", [P, 2, 2, S + 2], F32)]))
        B.update(over([("merged", [P, 8, S], F32)], (
            lambda: over([("sbq", [P, 8, S], F32)], (
                lambda: over([("sbk", [P, 8, S], F32), ("sbv", [P, 8, S], F32), ("sbvt", [P, TB, D], F32),
                              ("tz", [P, 1280], F32), ("ls", [P, 1280], F32), ("Lp", [P, 1280], F32)]),
                lambda: over([("oH", [P, 8, S], F32R), ("oL", [P, 8, S], F32R)]))),
            lambda: over([("gq", [P, 8, S], F32)], (
                lambda: over([("gk", [P, 8, S], F32), ("gv", [P, 8, S], F32)], (
                    lambda: over([("gpad", [P, 4, S + 4], F32)]),
                    lambda: over([("kw", [P, 4, P], F32), ("vb", [P, 4, P], F32), ("er", [P, 4, P], F32),
                              ("dT", [P, 4, P], F32), ("LT", [P, 4, P], F32), ("aT", [P, 4, P], F32),
                              ("Tm", [P, 4, P], F32), ("Rm", [P, 4, P], F32), ("Xm", [P, 4, P], F32),
                              ("Nm", [P, 4, P], F32), ("rhs", [P, 4, P], F32), ("state", [P, 8, P], F32),
                              ("ga", [P, 10, TB, 8], F32)]))),
                lambda: over([("goH", [P, 8, S], F32R), ("goL", [P, 8, S], F32R), ("gg", [P, 8, S], F32)]))))))
        B.update(over([("slots", [P, 3, S], F32)], (
            lambda: over([("qp", [P, 16, S], F32), ("keys", [P, 16, P], F32), ("work", [P, 256], F32),
                          ("cand", [P, 256], F32), ("v12", [P, 2, 16], F32), ("i12", [P, 8, 2, 16], U32),
                          ("cv", [P, 8, 16], F32), ("ci", [P, 8, 16], U32), ("cc", [P, 2, 8, 16], U32),
                          ("cf", [P, 2, 8, 16], F32), ("if12", [P, 8, 2, 16], F32), ("eq", [P, 2048], F32),
                          ("eg", [P, 4, P], F32)]),
            lambda: over([("onehot", [P, 2, 4, P], F32), ("gated", [P, 2, 4, P], F32),
                          ("stage", [P, 2, P, 32], F32)]))))
        B.update(over([("Gt", [P, TG, 8, 32], F32), ("pzH", [P, 8, S], F32R), ("pzL", [P, 8, S], F32R)]))

        gates = a["gates"]
        block = ctx.enter_context(nc.Block())
        n_loop = N_TILES // 4 * 4
        W = a["weights"]
        Wl = W[0:n_loop].rearrange("(j s) p f -> j s p f", s=4)

        ident, ones = C("ident"), C("ones")

        def freed(t):
            past = min(max(t - TILE["down"], 0), 22)
            return t // 2 - past // 2

        def tile_ready(E, t, j=None, per=0):
            E.eng.wait_ge(sems(f"tile_done{t % 2}"), t // 2 + 1 if j is None else t // 2 + 1 + per * j)

        def emptied(E, t, j=None, per=0):
            v = freed(t) + 1
            E.eng.wait_ge(sems(f"bank_free{t % 2}"), v if j is None else v + per * j)

        def empties(ins, t):
            ins.then_inc(sems(f"bank_free{t % 2}"), 1)

        def bank(t, w=S):
            return ps[t % 2][:, 0:w]


        def norm_act(E, groups, nk, src, nt=TB, split=False, **_):
            w = nt * P
            for g in range(groups):
                for k in range(nk):
                    i = E.made("sq")
                    E.at("sq_used", i - 3)
                    nc.scalar.activation(sq[:, i % 4, 0:w], src(g, k), ACT.Square).then_inc(sems("sq_ready"), 1)
            m = groups * nt
            E.wait("var_ready")
            nc.scalar.activation(st[:, 1, 0:m], st[:, 0, 0:m], ACT.Sqrt).then_inc(sems("std_ready"), 1)
            if split:
                for g in range(groups):
                    for k in range(nk):
                        hi_part(E, split(g, k)[0], w)

        def norm_pe(E, groups, nk, src, nt=TB, **_):
            w = nt * P
            E.at("var_ready", E.made("norm"))
            for g in range(groups):
                for k in range(nk):
                    E.wait("sq_ready")
                    i = E.made("sq")
                    for t in range(nt):
                        o = g * nt + t
                        mm = nc.tensor.matmul(ps[2][:, o:o + 1], sq[:, i % 4, t * P:(t + 1) * P], ones[:, 0:1],
                                              start=(g == 0 and k == 0 and t == 0), stop=True,
                                              skip_group_check=True)
                    mm.then_inc(sems("sq_used"), 1)
            for g in range(groups):
                i = E.made("rb")
                E.wait("diag_ready")
                E.at("rb_used", i - 1)
                nc.tensor.matmul(ps[3 + i % 2][:, 0:w], ones, dg[:, i % 2, 0:w],
                                          start=True, stop=True).then_inc(sems("rb_ready"), 1)

        def norm_dve(E, chain, groups, nk, src, gain, scale, nt=TB, split=None, dst=None):
            w = nt * P
            m = groups * nt
            v = nc.vector
            E.wait("sq_used", groups * nk)
            v.tensor_scalar(st[:, 0, 0:m], ps[2][:, 0:m], scale, EPS, ALU.mult, ALU.add).then_inc(sems("var_ready"), 1)
            E.wait("std_ready")
            chain(v.reciprocal(st[:, 2, 0:m], st[:, 1, 0:m]))
            chain(v.tensor_tensor(st[:, 3, 0:m], st[:, 2, 0:m], st[:, 2, 0:m], ALU.mult))
            chain(v.tensor_tensor(st[:, 3, 0:m], st[:, 3, 0:m], st[:, 0, 0:m], ALU.mult))
            chain(v.tensor_scalar(st[:, 3, 0:m], st[:, 3, 0:m], -0.5, 1.5, ALU.mult, ALU.add))
            chain(v.tensor_tensor(st[:, 4, 0:m], st[:, 2, 0:m], st[:, 3, 0:m], ALU.mult))

            def diagonal(g):
                i = E.made("diag")
                E.at("rb_ready", i - 1)
                v.tensor_tensor(dg[:, i % 2, 0:w].rearrange("p (a b) -> p a b", b=P),
                                         ident.unsqueeze(1).to_broadcast([P, nt, P]),
                                         st[:, 4, g * nt:(g + 1) * nt].unsqueeze(2).to_broadcast([P, nt, P]),
                                         ALU.mult).then_inc(sems("diag_ready"), 1)

            diagonal(0)
            held = []
            for g in range(groups):
                if g + 1 < groups:
                    diagonal(g + 1)
                E.wait("rb_ready")
                r = ps[3 + E.made("rbr") % 2][:, 0:w]
                for k in range(nk):
                    to = dst(g, k) if dst else None
                    if split:
                        if len(held) > 1:
                            lo_part(E, held.pop(0), w)
                        i = E.made("v")
                        to = tmp[:, i % 4, 0:w]
                        held.append((i, split(g, k)))
                    gn = gain(g, k)
                    if gn is None:
                        ins = v.tensor_tensor(to, src(g, k), r, ALU.mult)
                    else:
                        ins = v.scalar_tensor_tensor(out=to, in0=src(g, k), scalar=gn, in1=r,
                                                     op0=ALU.mult, op1=ALU.mult)
                    if split:
                        ins.then_inc(sems("v_ready"), 1)
                    elif k == nk - 1:
                        ins.then_inc(sems("rb_used"), 1)
                if split:
                    while held:
                        lo_part(E, held.pop(0), w, "rb_used" if len(held) == 0 else "lo_ready")

        def hi_part(E, H, w=S):
            E.wait("v_ready")
            i = E.made("v")
            nc.scalar.activation(H, tmp[:, i % 4, 0:w], ACT.Copy).then_inc(sems("hi_ready"), 1)

        def lo_part(E, what, w=S, name="lo_ready"):
            i, (H, L) = what
            E.wait("hi_ready")
            nc.vector.tensor_tensor(L, tmp[:, i % 4, 0:w], H.bitcast(F32), ALU.subtract).then_inc(sems(name), 1)

        HS = lambda g, k: (hH[:, k, :], hL[:, k, :])
        X = lambda g, k: xT[:, k, :]

        def main_norm(name):
            return dict(groups=1, nk=KB, src=X, gain=lambda g, k: PM(name, k), scale=1.0 / D, split=HS)

        NORMS = {
            "mem": dict(groups=1, nk=KB, nt=MB, src=lambda g, k: B["memT"][:, k, :],
                        gain=lambda g, k: PM("norm_mem", k), scale=1.0 / D,
                        split=lambda g, k: (hH[:, k, 0:NMEM], hL[:, k, 0:NMEM])),
            "mix": main_norm("norm_mix"), "cross": main_norm("norm_cross"), "ffn": main_norm("norm_ffn"),
            "final": dict(groups=1, nk=KB, src=X, gain=lambda g, k: PM("norm_final", k), scale=1.0 / D, dst=X),
            "mix2": main_norm("mix2"), "ffn2": main_norm("ffn2"),
            "heads": dict(groups=4, nk=1, src=lambda g, k: B["oT"][:, g, :], gain=lambda g, k: sc[:, 4:5],
                          scale=1.0 / P, split=lambda g, k: (hH[:, g, :], hL[:, g, :])),
            "ln": dict(groups=1, nk=4, src=lambda g, k: B["cacc"][:, k, :], gain=lambda g, k: PM("ln_g", k),
                       scale=1.0 / 512, dst=lambda g, k: B["cacc"][:, k, :]),
            "sb": dict(groups=16, nk=1, src=lambda g, k: B["sbq" if g < 8 else "sbk"][:, g % 8, :],
                       gain=lambda g, k: sc[:, 5:6] if g < 8 else PM("sbk"), scale=1.0 / P,
                       dst=lambda g, k: B["sbq" if g < 8 else "sbk"][:, g % 8, :]),
            "l2": dict(groups=16, nk=1, src=lambda g, k: B["gq" if g < 8 else "gk"][:, g % 8, :],
                       gain=lambda g, k: P ** -0.5 if g < 8 else None, scale=1.0,
                       dst=lambda g, k: B["gq" if g < 8 else "gk"][:, g % 8, :]),
            "gdn": dict(groups=8, nk=1, src=lambda g, k: B["gq"][:, g, :], gain=lambda g, k: PM("gdn_g"),
                        scale=1.0 / P, dst=lambda g, k: B["gq"][:, g, :]),
        }

        v = nc.vector
        act = nc.scalar

        offs = [0, 512, 896, 1152]
        qw = [S - P * kb for kb in range(TB)]

        def second_pe(E, products, one_tile, turn, h_hi, h_lo):
            pe = E.eng
            norm_pe(E, **NORMS["mix2"])
            E.meet()
            products("sb_qkv", 24, h_hi, h_lo)
            for b in range(8):
                emptied(E, TILE["sb_qkv"] + 16 + b)
                E.at("sbv_turned", b - 1)
                for t in range(TB):
                    mm = turn(ps[5 + b % 2][:, t * P:(t + 1) * P], B["sbv"][:, b, t * P:(t + 1) * P])
                mm.then_inc(sems("sbv_turn"), 1)
            E.meet()
            norm_pe(E, **NORMS["sb"])
            E.meet()
            for h in range(NH2):
                for kb in range(TB):
                    E.at("sb_L", TB * h)
                    if kb == 0:
                        E.at("sb_o_copied", h)
                    nc.tensor.matmul(ps[4 + kb][:, 0:qw[kb]], B["sbk"][:, h, kb * P:(kb + 1) * P],
                                              B["sbq"][:, h, kb * P:S], start=True, stop=True).then_inc(sems("sb_z"), 1)
                for kb in reversed(range(TB)):
                    E.wait("sb_L")
                    E.at("sb_la", TB * h)
                    mm = nc.tensor.matmul(ps[kb][:, 0:qw[kb]], C("low"), B["Lp"][:, offs[kb]:offs[kb] + qw[kb]],
                                          start=True, stop=True)
                    for later in range(kb + 1, TB):
                        mm = nc.tensor.matmul(ps[kb][:, P * (later - kb):qw[kb]], ones,
                                              B["Lp"][:, offs[later]:offs[later] + qw[later]],
                                              start=False, stop=True, skip_group_check=True)
                    mm.then_inc(sems("sb_S"), 1)
                for kb in range(TB):
                    E.at("sb_am", TB * h + TB)
                    mm = nc.tensor.matmul(ps[4][:, P * kb:S], B["sbvt"][:, kb, h * P:(h + 1) * P],
                                          B["tz"][:, offs[kb]:offs[kb] + qw[kb]], start=(kb == 0), stop=True,
                                          skip_group_check=True)
                mm.then_inc(sems("sb_o"), 1)
            E.meet()
            E.meet()
            products("gate_sb", 8, h_hi, h_lo)
            products("branch_sb", 8, lambda k: B["oH"][:, k, :], lambda k: B["oL"][:, k, :])
            E.meet()
            products("gdn_qkv", 24, h_hi, h_lo)
            products("ba", 1, h_hi, h_lo)
            E.meet()
            norm_pe(E, **NORMS["l2"])
            for t in range(TB):
                mm = turn(ps[5][:, t * P:(t + 1) * P], tmp[:, 0, t * P:(t + 1) * P])
            mm.then_inc(sems("ba_turned"), 1)
            E.wait("g_ready")
            pe.matmul(ps[6][:, 0:32], C("upi"), B["ga"][:, 1], start=True, stop=True)
            pe.matmul(ps[6][:, 32:64], ones, B["ga"][:, 1], start=True, stop=True).then_inc(sems("g_sums"), 1)
            E.meet()
            for n in range(2 * TB):
                tb, h0 = n // 2, 4 * (n % 2)
                ts = slice(tb * P, (tb + 1) * P)
                col = lambda x: slice(x * P, (x + 1) * P)
                E.at("gd_end", n)
                for x in range(4):
                    turn(ps[0][:, col(x)], B["gk"][:, h0 + x, ts])
                for x in range(4):
                    mm = turn(ps[1][:, col(x)], B["gv"][:, h0 + x, ts])
                mm.then_inc(sems("gd_turned"), 1)
                for x in range(4):
                    pe.matmul(ps[2][:, col(x)], B["gk"][:, h0 + x, ts], B["gk"][:, h0 + x, ts], start=True, stop=True)
                for x in range(4):
                    mm = pe.matmul(ps[3][:, col(x)], B["gk"][:, h0 + x, ts], B["gq"][:, h0 + x, ts], start=True, stop=True)
                mm.then_inc(sems("gd_kk"), 1)
                E.wait("gd_diag")
                pe.matmul(ps[4][:, :], ones, dg[:, 0, :], start=True, stop=True).then_inc(sems("gd_rows"), 1)
                E.wait("gd_diag")
                pe.matmul(ps[5][:, :], ones, dg[:, 1, :], start=True, stop=True).then_inc(sems("gd_rows"), 1)
                for lv in range(7):
                    E.wait("gd_N")
                    for x in range(4):
                        mm = pe.matmul(ps[6][:, col(x)], B["Nm"][:, x], B["Tm"][:, x], start=True, stop=True)
                    mm.then_inc(sems("gd_X"), 1)
                    E.wait("gd_Xc")
                    for x in range(4):
                        mm = pe.matmul(ps[7][:, col(x)], B["Rm"][:, x], B["Xm"][:, x], start=True, stop=True)
                    mm.then_inc(sems("gd_Y"), 1)
                    for x in range(4):
                        mm = pe.matmul(ps[6][:, col(x)], B["Xm"][:, x], B["Rm"][:, x], start=True, stop=True)
                    mm.then_inc(sems("gd_Y"), 1)
                for x in range(4):
                    mm = pe.matmul(ps[2][:, col(x)], B["gk"][:, h0 + x, ts], B["state"][:, h0 + x], start=True, stop=True)
                mm.then_inc(sems("gd_kS"), 1)
                E.wait("gd_rhs")
                for x in range(4):
                    mm = pe.matmul(ps[3][:, col(x)], B["Rm"][:, x], B["rhs"][:, x], start=True, stop=True)
                mm.then_inc(sems("gd_v"), 1)
                E.wait("gd_vc")
                for x in range(4):
                    pe.matmul(ps[4][:, col(x)], B["state"][:, h0 + x], B["er"][:, x], start=True, stop=False)
                    mm = pe.matmul(ps[4][:, col(x)], B["Xm"][:, x], B["aT"][:, x], start=False, stop=True)
                mm.then_inc(sems("gd_o"), 1)
                for x in range(4):
                    mm = pe.matmul(ps[5][:, col(x)], B["kw"][:, x], B["Xm"][:, x], start=True, stop=True)
                mm.then_inc(sems("gd_S"), 1)
            E.meet()
            norm_pe(E, **NORMS["gdn"])
            E.meet()
            products("z", 8, h_hi, h_lo)
            products("gate_gdn", 8, h_hi, h_lo)
            E.at("gz_done", 8)
            products("branch_gdn", 8, lambda k: B["goH"][:, k, :], lambda k: B["goL"][:, k, :])
            E.meet()
            E.meet()
            products("out2", 8, h_hi, h_lo)
            E.meet()
            norm_pe(E, **NORMS["ffn2"])
            E.meet()
            products("wq", 16, h_hi, h_lo)
            E.meet()
            pe.wait_ge(sems("keys_in"), 16)
            for u in range(32):
                tb, h = u // 8, u % 8
                E.at("tk_read", 2 * (u - 1))
                for c in range(2):
                    mm = pe.matmul(ps[2 + u % 2][:, c * P:(c + 1) * P], B["qp"][:, 2 * h + c, tb * P:(tb + 1) * P],
                                   B["keys"][:, 2 * h + c, :], start=True, stop=True)
                mm.then_inc(sems("tk_scores"), 1)
                if h == 7:
                    for c in range(3):
                        E.wait("tk_expert")
                        E.at("slots_copied", 3 * tb + c)
                        turn(ps[4][:, 0:P], B["eg"][:, c]).then_inc(sems("slots_turned"), 1)
            E.meet()
            E.prime("gb_product")
            with pe.Fori(0, TG) as j:
                for r in range(8):
                    pe.wait_ge(sems("gb_rows"), 8 * j + (r + 1))
                    pe.wait_ge(sems("gb_copied"), 8 * j + max(r, 1))
                    for x in range(4):
                        mm = pe.matmul(ps[2 + r % 2][:, x * P:(x + 1) * P], B["gated"][:, r % 2, x], B["onehot"][:, r % 2, x],
                                       start=True, stop=True)
                    mm.then_inc(sems("gb_product"), 1)
            E.meet()
            t0 = TILE["peer"]
            with pe.Fori(0, GROUPS) as j:
                for e in range(8):
                    one_tile(t0 + e, h_hi, h_lo, S, j, 16)
                for d in range(8):
                    def weighed(k):
                        if d == 0:
                            pe.wait_ge(sems("pz_ready"), 8 * j + (k + 2))
                    one_tile(t0 + 8 + d, lambda k: B["pzH"][:, k, :], lambda k: B["pzL"][:, k, :], S, j, 16, ready=weighed)
            E.meet()

        def second_act(E, eng, copy_tiles):
            if not first:
                eng.wait_ge(sems("x_in"), 16)
            norm_act(E, **NORMS["mix2"])
            E.meet()
            for n, name in enumerate(("sbq", "sbk", "sbv")):
                copy_tiles("sb_qkv", 8, lambda b: B[name][:, b, :], at=8 * n)
            E.meet()
            norm_act(E, **NORMS["sb"])
            E.meet()
            for h in range(NH2):
                for kb in range(TB):
                    E.wait("sb_z")
                    E.at("sb_o", h)
                    act.activation(B["tz"][:, offs[kb]:offs[kb] + qw[kb]], ps[4 + kb][:, 0:qw[kb]], ACT.Abs).then_inc(sems("sb_step"), 1)
                E.wait("sb_step", 4)
                act.activation(B["tz"][:], B["tz"][:], ACT.Exp, scale=-1.0).then_inc(sems("sb_step"), 1)
                E.wait("sb_step")
                act.activation(B["tz"][:], B["tz"][:], ACT.Ln, bias=1.0).then_inc(sems("sb_t"), 1)
                for kb in reversed(range(TB)):
                    E.wait("sb_la")
                    E.at("sb_L", TB * h + TB)
                    o = slice(offs[kb], offs[kb] + qw[kb])
                    act.activation(B["tz"][:, o], B["ls"][:, o], ACT.Exp).then_inc(sems("sb_a"), 1)
                E.wait("sb_o")
                act.activation(B["sbq"][:, h, :], ps[4][:, :], ACT.Copy).then_inc(sems("sb_o_copied"), 1)
            E.meet()
            for h in range(NH2):
                act.activation(B["oH"][:, h, :], B["sbq"][:, h, :], ACT.Copy).then_inc(sems("hi_ready"), 1)
            E.meet()
            copy_tiles("gate_sb", 8, lambda b: B["merged"][:, b, :], func=ACT.Sigmoid)
            E.meet()
            for i in range(25):
                if i < 24:
                    t = TILE["gdn_qkv"] + i
                    tile_ready(E, t)
                    E.at("gconv", i - 3)
                    empties(act.activation(B["gpad"][:, i % 4, 3:S + 3], bank(t), ACT.Copy), t)
                if 1 <= i <= 24:
                    E.at("gconv", i)
                    to = B[("gq", "gk", "gv")[(i - 1) // 8]][:, (i - 1) % 8, :]
                    act.activation(to, to, ACT.Silu)
            copy_tiles("ba", 1, lambda b: tmp[:, 0, :])
            E.meet()
            norm_act(E, **NORMS["l2"])
            ga = lambda n: B["ga"][:, n]
            E.wait("ba_raw")
            act.activation(ga(0), ga(8), ACT.Sigmoid).then_inc(sems("ga_act"), 1)
            act.activation(ga(2), ga(9), ACT.Abs).then_inc(sems("ga_step"), 1)
            E.wait("ga_step")
            act.activation(ga(2), ga(2), ACT.Exp, scale=-1.0).then_inc(sems("ga_step"), 1)
            E.wait("ga_step")
            act.activation(ga(2), ga(2), ACT.Ln, bias=1.0)
            act.activation(sc[:, 8:16], PM("a_log", 0, 8), ACT.Exp).then_inc(sems("ga_act"), 1)
            E.wait("gc_ready")
            act.activation(ga(3), ga(2), ACT.Exp)
            act.activation(ga(6), ga(5), ACT.Exp)
            act.activation(ga(7), ga(4), ACT.Exp).then_inc(sems("ga_act"), 1)
            E.meet()
            for n in range(2 * TB):
                tb, h0 = n // 2, 4 * (n % 2)
                ts = slice(tb * P, (tb + 1) * P)
                E.at("gd_rows", 2 * n + 1)
                E.at("gd_end", n)
                act.activation(B["er"][:], ps[4][:, :].rearrange("p (x t) -> p x t", x=4), ACT.Exp).then_inc(sems("gd_er"), 1)
                E.wait("gd_dT")
                act.activation(B["dT"][:], B["dT"][:], ACT.Exp).then_inc(sems("gd_dTe"), 1)
                for lv in range(7):
                    E.wait("gd_X")
                    act.activation(B["Xm"][:], ps[6][:, :].rearrange("p (x t) -> p x t", x=4), ACT.Copy).then_inc(sems("gd_Xc"), 1)
                E.wait("gd_v")
                act.activation(B["Xm"][:], ps[3][:, :].rearrange("p (x t) -> p x t", x=4), ACT.Copy).then_inc(sems("gd_vc"), 1)
            E.meet()
            norm_act(E, **NORMS["gdn"])
            E.meet()
            for b in range(8):
                t = TILE["z"] + b
                tile_ready(E, t)
                E.at("gz", b - 3)
                empties(act.activation(sq[:, b % 4, :], bank(t), ACT.Silu), t)
                E.at("gz", b + 1)
                act.activation(B["goH"][:, b, :], B["gq"][:, b, :], ACT.Copy).then_inc(sems("hi_ready"), 1)
            copy_tiles("gate_gdn", 8, lambda b: B["gg"][:, b, :], func=ACT.Sigmoid)
            E.meet()
            for b in range(8):
                act.activation(hH[:, b, :], B["merged"][:, b, :], ACT.Copy).then_inc(sems("hi_ready"), 1)
            E.meet()
            E.meet()
            norm_act(E, **NORMS["ffn2"])
            eng.dma_start(B["keys"][:], a["keys"].rearrange("n d k -> d n k")).then_inc(sems("keys_in"), 16)
            E.meet()
            copy_tiles("wq", 16, lambda b: B["qp"][:, b, :])
            E.meet()
            for tb in range(TB):
                E.wait("tk_centred")
                act.activation(B["cv"][:], B["cv"][:], ACT.Exp).then_inc(sems("tk_exp"), 1)
                for c in range(3):
                    E.wait("slots_turned")
                    act.activation(B["slots"][:, c, tb * P:(tb + 1) * P], ps[4][:, 0:P], ACT.Copy).then_inc(sems("slots_copied"), 1)
            E.meet()
            E.prime("gb_copied")
            for jj in range(2):
                E.prime(f"stage_out{jj}", 16)
            with eng.Fori(0, TG // 2) as j:
                for jj in range(2):
                    for r in range(8):
                        eng.wait_ge(sems("gb_product"), 16 * j + (8 * jj + r + 2))
                        if r == 0:
                            eng.wait_ge(sems(f"stage_out{jj}"), 16 * j + 16)
                        ins = act.activation(B["stage"][:, jj, :, 4 * r:4 * r + 4].rearrange("p e t -> p t e"),
                                             ps[2 + r % 2][:, :].rearrange("p (t e) -> p t e", t=4), ACT.Copy)
                        ins.then_inc(sems("gb_copied"), 1)
                    eng.wait_ge(sems("gb_copied"), 16 * j + (8 * jj + 9))
                    eng.dma_start(gates.rearrange("(j s) p e t -> j s p (e t)", s=2)[bass.ds(j, 1), jj].rearrange("o p f -> p (o f)"),
                                  B["stage"][:, jj].rearrange("p e t -> p (e t)")).then_inc(sems(f"stage_out{jj}"), 16)
            for jj in range(2):
                eng.wait_ge(sems(f"stage_out{jj}"), 16 * (TG // 2) + 16)
            E.meet()
            t0 = TILE["peer"]
            with eng.Fori(0, GROUPS) as j:
                eng.wait_ge(sems("pz_v"), 8 * j + 1)
                eng.dma_start(B["Gt"][:], gates.rearrange("g p (n e) t -> n p g (e t)", e=8)[bass.ds(j, 1)].rearrange(
                    "o p g f -> p (o g) f")).then_inc(sems("gates_in"), 16)
                for e in range(8):
                    t = t0 + e
                    tile_ready(E, t, j, 8)
                    n = 8 * j + e
                    if e >= 2:
                        eng.wait_ge(sems("pz_v"), n)
                    act.activation(sq[:, e % 2, :], bank(t), ACT.Gelu).then_inc(sems(f"bank_free{t % 2}"), 1)
                    if e >= 1:
                        eng.wait_ge(sems("pz_v"), n + 1)
                        act.activation(B["pzH"][:, e - 1, :], tmp[:, (e - 1) % 4, :], ACT.Copy).then_inc(sems("pz_hi"), 1)
                eng.wait_ge(sems("pz_v"), 8 * j + 9)
                act.activation(B["pzH"][:, 7, :], tmp[:, 3, :], ACT.Copy).then_inc(sems("pz_hi"), 1)
            E.meet()

        def second_dve(E, eng, chain, add_tiles):
            chain(v.tensor_scalar(sc[:, 5:6], PM("sbq"), P ** -0.5, None, ALU.mult))
            if not first:
                eng.wait_ge(sems("x_in"), 16)
            norm_dve(E, chain, **NORMS["mix2"])
            E.meet()
            for b in range(8):
                E.wait("sbv_turn")
                v.tensor_copy(B["sbvt"][:, :, b * P:(b + 1) * P],
                                       ps[5 + b % 2][:, :].rearrange("p (t d) -> p t d", t=TB)).then_inc(sems("sbv_turned"), 1)
            E.meet()
            norm_dve(E, chain, **NORMS["sb"])
            E.meet()
            for h in range(NH2):
                E.wait("sb_t")
                for kb in reversed(range(TB)):
                    o = slice(offs[kb], offs[kb] + qw[kb])
                    z = ps[4 + kb][:, 0:qw[kb]]
                    E.at("sb_a", TB * h)
                    chain(v.scalar_tensor_tensor(out=B["ls"][:, o], in0=z, scalar=0.0, in1=B["tz"][:, o], op0=ALU.min, op1=ALU.subtract))
                    E.at("sb_S", TB * h)
                    chain(v.scalar_tensor_tensor(out=B["Lp"][:, o], in0=z, scalar=0.0, in1=B["tz"][:, o], op0=ALU.max, op1=ALU.add))
                    d = slice(offs[kb], offs[kb] + P)
                    v.tensor_tensor(B["Lp"][:, d], B["Lp"][:, d], C("ups"), ALU.mult).then_inc(sems("sb_L"), 1)
                for kb in reversed(range(TB)):
                    o = slice(offs[kb], offs[kb] + qw[kb])
                    E.wait("sb_S")
                    v.tensor_tensor(B["ls"][:, o], B["ls"][:, o], ps[kb][:, 0:qw[kb]], ALU.subtract).then_inc(sems("sb_la"), 1)
                for kb in reversed(range(TB)):
                    d = slice(offs[kb], offs[kb] + P)
                    E.wait("sb_a")
                    v.tensor_tensor(B["tz"][:, d], B["tz"][:, d], C("ups"), ALU.mult).then_inc(sems("sb_am"), 1)
            E.meet()
            for h in range(NH2):
                E.wait("hi_ready")
                v.tensor_tensor(B["oL"][:, h, :], B["sbq"][:, h, :], B["oH"][:, h, :].bitcast(F32), ALU.subtract).then_inc(sems("lo_ready"), 1)
            E.meet()
            for b in range(8):
                t = TILE["branch_sb"] + b
                tile_ready(E, t)
                emptied(E, TILE["gate_sb"] + b)
                empties(v.tensor_tensor(B["merged"][:, b, :], B["merged"][:, b, :], bank(t), ALU.mult), t)
            E.meet()
            chain(v.memset(B["gpad"][:, :, 0:3], 0.0))
            for i in range(24):
                emptied(E, TILE["gdn_qkv"] + i)
                u = B["gpad"][:, i % 4, :]
                to = B[("gq", "gk", "gv")[i // 8]][:, i % 8, :]
                w = lambda k: PM("gdn_w", 4 * i + k)
                chain(v.tensor_scalar(to, u[:, 0:S], w(0), None, ALU.mult))
                for k in range(1, 4):
                    ins = v.scalar_tensor_tensor(out=to, in0=u[:, k:S + k], scalar=w(k), in1=to, op0=ALU.mult, op1=ALU.add)
                    if k < 3:
                        chain(ins)
                ins.then_inc(sems("gconv"), 1)
            E.meet()
            norm_dve(E, chain, **NORMS["l2"])
            ga = lambda n: B["ga"][:, n]
            E.wait("ba_turned")
            bt = ps[5][:, :].rearrange("p (t c) -> p t c", t=TB)
            chain(v.tensor_copy(ga(8), bt[:, :, 0:8]))
            v.tensor_tensor(ga(9), bt[:, :, 8:16], PM("dt", 0, 8).unsqueeze(1).to_broadcast([P, TB, 8]), ALU.add).then_inc(sems("ba_raw"), 1)
            E.wait("ga_act", 2)
            E.at("ba_raw", 1)
            chain(v.scalar_tensor_tensor(out=ga(9), in0=ga(9), scalar=0.0, in1=ga(2), op0=ALU.max, op1=ALU.add))
            v.scalar_tensor_tensor(out=ga(1), in0=ga(9), scalar=-1.0, in1=sc[:, 8:16].unsqueeze(1).to_broadcast([P, TB, 8]),
                                            op0=ALU.mult, op1=ALU.mult).then_inc(sems("g_ready"), 1)
            E.wait("g_sums")
            sums = lambda n: ps[6][:, 32 * n:32 * n + 32].rearrange("p (t h) -> p t h", t=TB)
            chain(v.tensor_copy(ga(2), sums(0)))
            chain(v.tensor_copy(ga(4), sums(1)))
            v.tensor_tensor(ga(5), ga(4), ga(2), ALU.subtract).then_inc(sems("gc_ready"), 1)
            E.wait("ga_act")
            chain(v.scalar_tensor_tensor(out=ga(8), in0=ga(3), scalar=-1.0, in1=ga(0), op0=ALU.mult, op1=ALU.mult))
            chain(v.memset(B["state"][:], 0.0))
            E.meet()
            bc = [P, 4, P]
            for n in range(2 * TB):
                tb, h0 = n // 2, 4 * (n % 2)
                ts = slice(tb * P, (tb + 1) * P)
                gs = lambda m: B["ga"][:, m, tb, h0:h0 + 4].unsqueeze(2).to_broadcast(bc)
                bank4 = lambda m: ps[m][:, :].rearrange("p (x t) -> p x t", x=4)
                d4 = lambda m: dg[:, m, :].rearrange("p (x t) -> p x t", x=4)
                wide = lambda ap: ap.unsqueeze(1).to_broadcast(bc)
                if n:
                    E.at("gd_S", n)
                v.tensor_tensor(d4(0), wide(C("upi")), gs(1), ALU.mult).then_inc(sems("gd_diag"), 1)
                v.tensor_tensor(d4(1), wide(ident), gs(0), ALU.mult).then_inc(sems("gd_diag"), 1)
                E.wait("gd_turned")
                chain(v.tensor_tensor(B["kw"][:], bank4(0), gs(6), ALU.mult))
                chain(v.tensor_tensor(B["vb"][:], bank4(1), gs(0), ALU.mult))
                E.wait("gd_er")
                chain(v.tensor_tensor(B["dT"][:], bank4(4), gs(2), ALU.subtract))
                v.tensor_scalar(B["dT"][:], B["dT"][:], 0.0, None, ALU.min).then_inc(sems("gd_dT"), 1)
                chain(v.tensor_tensor(B["er"][:], B["er"][:], B["gq"][:, h0:h0 + 4, ts], ALU.mult))
                E.wait("gd_kk")
                E.wait("gd_dTe")
                chain(v.tensor_tensor(B["LT"][:], bank4(2), B["dT"][:], ALU.mult))
                chain(v.tensor_tensor(B["aT"][:], bank4(3), B["dT"][:], ALU.mult))
                chain(v.tensor_tensor(B["LT"][:], B["LT"][:], wide(C("ups")), ALU.mult))
                chain(v.tensor_tensor(B["aT"][:], B["aT"][:], wide(C("upi")), ALU.mult))
                E.wait("gd_rows", 2)
                chain(v.tensor_tensor(B["LT"][:], B["LT"][:], bank4(5), ALU.mult))
                chain(v.tensor_copy(B["Tm"][:], wide(ident)))
                chain(v.tensor_copy(B["Rm"][:], wide(ident)))
                for lv in range(7):
                    v.tensor_tensor(B["Nm"][:], B["LT"][:], wide(C("levels", lv * P, P)), ALU.mult).then_inc(sems("gd_N"), 1)
                    E.wait("gd_Y", 2)
                    chain(v.tensor_tensor(B["Tm"][:], B["Tm"][:], bank4(7), ALU.subtract))
                    chain(v.tensor_tensor(B["Rm"][:], B["Rm"][:], bank4(6), ALU.subtract))
                E.wait("gd_kS")
                chain(v.tensor_tensor(B["rhs"][:], bank4(2), gs(8), ALU.mult))
                v.tensor_tensor(B["rhs"][:], B["rhs"][:], B["vb"][:], ALU.add).then_inc(sems("gd_rhs"), 1)
                E.wait("gd_o")
                chain(v.tensor_copy(B["gq"][:, h0:h0 + 4, ts], bank4(4)))
                E.wait("gd_S")
                st8 = B["state"][:, h0:h0 + 4]
                chain(v.tensor_tensor(st8, st8, gs(7), ALU.mult))
                v.tensor_tensor(st8, st8, bank4(5), ALU.add).then_inc(sems("gd_end"), 1)
            E.meet()
            norm_dve(E, chain, **NORMS["gdn"])
            E.meet()
            for b in range(8):
                emptied(E, TILE["z"] + b)
                v.tensor_tensor(B["gq"][:, b, :], B["gq"][:, b, :], sq[:, b % 4, :], ALU.mult).then_inc(sems("gz"), 1)
                E.wait("hi_ready")
                v.tensor_tensor(B["goL"][:, b, :], B["gq"][:, b, :], B["goH"][:, b, :].bitcast(F32), ALU.subtract).then_inc(sems("gz_done"), 1)
            for b in range(8):
                t = TILE["branch_gdn"] + b
                tile_ready(E, t)
                emptied(E, TILE["gate_gdn"] + b)
                empties(v.tensor_tensor(tmp[:, b % 4, :], bank(t), B["gg"][:, b, :], ALU.mult), t)
                emptied(E, t)
                chain(v.tensor_tensor(B["merged"][:, b, :], B["merged"][:, b, :], tmp[:, b % 4, :], ALU.add))
            E.meet()
            for b in range(8):
                E.wait("hi_ready")
                v.tensor_tensor(hL[:, b, :], B["merged"][:, b, :], hH[:, b, :].bitcast(F32), ALU.subtract).then_inc(sems("lo_ready"), 1)
            E.meet()
            add_tiles("out2")
            E.meet()
            norm_dve(E, chain, **NORMS["ffn2"])
            E.meet()
            E.meet()
            u8 = lambda o: slice(8 * o, 8 * o + 8)
            for u in range(32):
                tb, h = u // 8, u % 8
                E.wait("tk_scores")
                for c in range(2):
                    s = ps[2 + u % 2][:, c * P:(c + 1) * P]
                    vals, idx = B["v12"][:, c], B["i12"][:, h, c]
                    wk = B["work"][:, c * P:(c + 1) * P]
                    chain(v.max(vals[:, u8(0)], s))
                    chain(v.max_index(idx[:, u8(0)], vals[:, u8(0)], s))
                    v.match_replace(wk, vals[:, u8(0)], s, NEG * 1e8).then_inc(sems("tk_read"), 1)
                    E.at("tk_read", 2 * u + c + 1)
                    chain(v.max(vals[:, u8(1)], wk))
                    chain(v.max_index(idx[:, u8(1)], vals[:, u8(1)], wk))
                cand = B["cand"][:].rearrange("p (i j) -> p i j", i=16)
                chain(v.tensor_tensor(cand, B["v12"][:, 0].unsqueeze(2).to_broadcast([P, 16, 16]),
                                      B["v12"][:, 1].unsqueeze(1).to_broadcast([P, 16, 16]), ALU.add))
                cv, ci = B["cv"][:, h], B["ci"][:, h]
                if h == 0 and tb:
                    E.at("slots_turned", 3 * tb)
                chain(v.max(cv[:, u8(0)], B["cand"][:]))
                chain(v.max_index(ci[:, u8(0)], cv[:, u8(0)], B["cand"][:]))
                chain(v.match_replace(B["work"][:], cv[:, u8(0)], B["cand"][:], NEG * 1e8))
                chain(v.max(cv[:, u8(1)], B["work"][:]))
                chain(v.max_index(ci[:, u8(1)], cv[:, u8(1)], B["work"][:]))
                if h < 7:
                    continue
                chain(v.tensor_single_scalar(B["cc"][:, 0], B["ci"][:], 4, ALU.logical_shift_right))
                chain(v.tensor_single_scalar(B["cc"][:, 1], B["ci"][:], 15, ALU.bitwise_and))
                chain(v.tensor_copy(B["cf"][:], B["cc"][:]))
                chain(v.tensor_copy(B["if12"][:], B["i12"][:]))
                eq = B["eq"][:].rearrange("p (n i) -> p n i", i=16)
                for c in range(2):
                    E.at("tk_expert", 3 * tb + c)
                    chain(v.tensor_tensor(eq, B["cf"][:, c].rearrange("p h s -> p (h s)").unsqueeze(2).to_broadcast([P, P, 16]),
                                          C("iota", 0, 16).unsqueeze(1).to_broadcast([P, P, 16]), ALU.is_equal))
                    e4 = B["eq"][:].rearrange("p (h s i) -> p h s i", h=8, i=16)
                    chain(v.tensor_tensor(e4, e4, B["if12"][:, :, c].unsqueeze(2).to_broadcast([P, 8, 16, 16]), ALU.mult))
                    v.tensor_reduce(B["eg"][:, c], eq, AX, ALU.add).then_inc(sems("tk_expert"), 1)
                cvs = B["cv"][:]
                chain(v.tensor_copy(B["eg"][:, 3, 0:8], B["cv"][:, :, 0]))
                v.tensor_tensor(cvs, cvs, B["eg"][:, 3, 0:8].unsqueeze(2).to_broadcast([P, 8, 16]), ALU.subtract).then_inc(sems("tk_centred"), 1)
                E.wait("tk_exp")
                chain(v.tensor_reduce(B["eg"][:, 3, 8:16], cvs, AX, ALU.add))
                chain(v.reciprocal(B["eg"][:, 3, 16:24], B["eg"][:, 3, 8:16]))
                v.tensor_tensor(B["eg"][:, 2].rearrange("p (h s) -> p h s", h=8), cvs,
                                         B["eg"][:, 3, 16:24].unsqueeze(2).to_broadcast([P, 8, 16]), ALU.mult).then_inc(sems("tk_expert"), 1)
            E.meet()
            with eng.Fori(0, TG) as j:
                e1 = B["slots"][:, 0].rearrange("p (j r x) -> p j r x", j=TG, x=4)
                for r in range(8):
                    eng.wait_ge(sems("gb_product"), 8 * j + max(r, 1))
                    v.tensor_tensor(B["onehot"][:, r % 2], C("iota").unsqueeze(1).to_broadcast(bc),
                                    e1[:, bass.ds(j, 1), r].rearrange("p o x -> p (o x)").unsqueeze(2).to_broadcast(bc), ALU.is_equal)
                    for x in range(4):
                        at = lambda c: B["slots"][:, c].rearrange("p (j n) -> p j n", j=TG)[:, bass.ds(j, 1), 4 * r + x]
                        ins = v.tensor_scalar(B["gated"][:, r % 2, x], C("iota"), at(1), at(2), ALU.is_equal, ALU.mult)
                    ins.then_inc(sems("gb_rows"), 1)
            E.meet()
            t0 = TILE["peer"]
            E.prime("pz_v")
            E.prime("pz_ready")
            with eng.Fori(0, GROUPS) as j:
                eng.wait_ge(sems("gates_in"), 16 * j + 16)
                eng.wait_ge(sems("pz_ready"), 8 * j + 1)
                for e in range(9):
                    n = 8 * j + e
                    if e < 8:
                        emptied(E, t0 + e, j, 8)
                        if e >= 4:
                            eng.wait_ge(sems("pz_ready"), n - 2)
                        v.tensor_tensor(tmp[:, e % 4, :].rearrange("p (g t) -> p g t", g=TG),
                                        sq[:, e % 2, :].rearrange("p (g t) -> p g t", g=TG), B["Gt"][:, :, e, :],
                                        ALU.mult).then_inc(sems("pz_v"), 1)
                    if e >= 1:
                        eng.wait_ge(sems("pz_hi"), n)
                        v.tensor_tensor(B["pzL"][:, e - 1, :], tmp[:, (e - 1) % 4, :], B["pzH"][:, e - 1, :].bitcast(F32),
                                        ALU.subtract).then_inc(sems("pz_ready"), 1)
                for d in range(8):
                    t = t0 + 8 + d
                    tile_ready(E, t, j, 8)
                    v.tensor_tensor(xT[:, d, :], xT[:, d, :], bank(t), ALU.add).then_inc(sems(f"bank_free{t % 2}"), 1)
            E.meet()


        ENGINES = ("pe", "act", "dve")

        def side(eng, me):
            return Side(eng, sems, f"{me}_idle", [f"{o}_idle" for o in ENGINES if o != me])

        @block.sync
        def _(sp):
            sp.dma_start(cst[:], a["consts"]).then_inc(sems("consts_in"), 16)
            sp.dma_start(par[:], a["params"]).then_inc(sems("consts_in"), 16)
            if first:
                sp.dma_start(B["memT"][:], a["memT"].rearrange("(k p) t -> p k t", p=P)).then_inc(sems("mem_in"), 16)
            sp.dma_start(xT[:], a["xT"].rearrange("(k p) t -> p k t", p=P)).then_inc(sems("x_in"), 16)
            for s in range(4):
                sp.dma_start(raw[:, s, :], Wl[0, s]).then_inc(sems(f"raw_in{s}"), 16)
            with sp.Fori(1, n_loop // 4) as j:
                for s in range(4):
                    sp.wait_ge(sems("weights_split"), 4 * j + (s - 3))
                    sp.dma_start(raw[:, s, :], Wl[bass.ds(j, 1), s].rearrange("o p f -> p (o f)")).then_inc(
                        sems(f"raw_in{s}"), 16)
            for t in range(n_loop, N_TILES):
                sp.wait_ge(sems("weights_split"), t - 3)
                sp.dma_start(raw[:, t % 4, :], W[t]).then_inc(sems(f"raw_in{t % 4}"), 16)

        @block.gpsimd
        def _(pool):
            nc.gpsimd.memset(cell[:], 0.0).then_inc(sems("cell_clear"), 1)
            pool.wait_ge(sems("cell_clear"), 1)

            def split_tile(s, t, landed, used, done):
                pool.wait_ge(sems(f"raw_in{s}"), landed)
                if t is None or t >= 2:
                    pool.wait_ge(sems(f"tile_done{s % 2}"), used)
                nc.gpsimd.tensor_tensor(cell[:, 0:1], cell[:, 1:2], cell[:, 1:2], ALU.add)
                nc.gpsimd.tensor_scalar(wH[:, s % 2, :], raw[:, s, :], 1.0, 0.0, ALU.mult, ALU.add).then_inc(
                    sems("weights_hi"), 1)
                pool.wait_ge(sems("weights_hi"), done)
                nc.gpsimd.tensor_tensor(wL[:, s % 2, :], raw[:, s, :], wH[:, s % 2, :].bitcast(F32),
                                        ALU.subtract).then_inc(sems("weights_split"), 1)

            for s in range(4):
                split_tile(s, s, 16, s // 2, s + 1)
            with pool.Fori(1, n_loop // 4) as j:
                for s in range(4):
                    split_tile(s, None, 16 * j + 16, 2 * j + s // 2, 4 * j + (s + 1))
            for t in range(n_loop, N_TILES):
                split_tile(t % 4, t, 16 * (t // 4) + 16, t // 2, t + 1)

        @block.tensor
        def _(pe):
            E = side(pe, "pe")

            def three(out, w, H, L, k, w_slot, start, stop):
                c = slice(P * k, P * k + P)
                pe.matmul(out, wH[:, w_slot, c], H, start=start, stop=False)
                pe.matmul(out, wH[:, w_slot, c], L, start=False, stop=False)
                return pe.matmul(out, wL[:, w_slot, c], H, start=False, stop=stop)

            def one_tile(t, H, L, w=S, j=None, step=0, ready=None):
                def plus(n, per):
                    return n if j is None else n + per * j
                pe.wait_ge(sems("weights_split"), plus(t + 1, step))
                if t >= 2 or j is not None:
                    pe.wait_ge(sems(f"bank_free{t % 2}"), plus(freed(t), step // 2))
                for k in range(8):
                    if ready:
                        ready(k)
                    mm = three(bank(t, w), w, H(k), L(k), k, t % 2, k == 0, k == 7)
                mm.then_inc(sems(f"tile_done{t % 2}"), 1)

            def products(name, n, H, L, w=S, at=0):
                t0 = TILE[name] + at
                if n >= 4:
                    if t0 == 0:
                        one_tile(0, H, L, w)
                        one_tile(1, H, L, w)
                    with pe.Fori(1 if t0 == 0 else 0, n // 2) as j:
                        for s in range(2):
                            one_tile(t0 + s, H, L, w, j, 2)
                    for t in range(t0 + n // 2 * 2, t0 + n):
                        one_tile(t, H, L, w)
                else:
                    for t in range(t0, t0 + n):
                        one_tile(t, H, L, w)

            def turn(out, in_):
                return nc.tensor.transpose(out, in_, ident)

            h_hi = lambda k: hH[:, k, :]
            h_lo = lambda k: hL[:, k, :]
            pe.wait_ge(sems("consts_in"), 32)

            if first:
                norm_pe(E, **NORMS["mem"])
                E.meet()
                products("ckv", 8, lambda k: hH[:, k, 0:NMEM], lambda k: hL[:, k, 0:NMEM], NMEM)
                for b in range(8):
                    t = TILE["ckv"] + 8 + b
                    one_tile(t, lambda k: hH[:, k, 0:NMEM], lambda k: hL[:, k, 0:NMEM], NMEM)
                    emptied(E, t)
                    E.at("mem_turned", b - 1)
                    for m in range(MB):
                        mm = turn(ps[5 + b % 2][:, m * P:(m + 1) * P], tmp[:, b % 4, m * P:(m + 1) * P])
                    mm.then_inc(sems("mem_turn"), 1)
                E.meet()
                norm_pe(E, **NORMS["mix"])
                E.meet()
                products("in_u", 8, h_hi, h_lo)
                products("in_qkv", 12, h_hi, h_lo)
                for b in range(4):
                    emptied(E, TILE["in_qkv"] + 8 + b)
                    E.at("v_copied", b - 1)
                    for t in range(TB):
                        mm = turn(ps[5 + b % 2][:, t * P:(t + 1) * P], B["vT"][:, b, t * P:(t + 1) * P])
                    mm.then_inc(sems("v_turned"), 1)
                for b in range(8):
                    E.at("roped", b - 1)
                    nc.tensor.matmul(ps[3 + b % 2][:, :], C("swap"), B["qkT"][:, b, :], start=True,
                                              stop=True).then_inc(sems("swapped"), 1)
                E.meet()
                units = [(h, i) for h in range(4) for i in range(TB)]

                def scores(u):
                    h, i = units[u]
                    E.at("probs", 2 * (u - 1))
                    for c in range(2):
                        r = slice(64 * c, 64 * c + 64)
                        nc.tensor.matmul(ps[2 + 2 * (u % 2) + c][:, 0:P * (i + 1)],
                                                  B["qkT"][r, h, i * P:(i + 1) * P],
                                                  B["qkT"][r, 4 + h, 0:P * (i + 1)], start=True, stop=True).then_inc(sems("scores"), 1)

                scores(0)
                for u, (h, i) in enumerate(units):
                    if u + 1 < len(units):
                        scores(u + 1)
                    E.wait("att")
                    E.at("attT", u)
                    for kb in range(i + 1):
                        mm = turn(ps[6][:, kb * P:(kb + 1) * P], B["att"][:, u % 2, kb * P:(kb + 1) * P])
                    mm.then_inc(sems("att_turned"), 1)
                    E.at("attT", u + 1)
                    if i == 0:
                        E.at("oT", h)
                    for kb in range(i + 1):
                        mm = nc.tensor.matmul(ps[7][:, i * P:(i + 1) * P], B["vtok"][:, kb, h * P:(h + 1) * P],
                                              B["attT"][:, u % 2, kb * P:(kb + 1) * P], start=(kb == 0), stop=(kb == i))
                    mm.then_inc(sems("pv"), 1)
                E.meet()
                norm_pe(E, **NORMS["heads"])
                for k in range(4):
                    mm = nc.tensor.matmul(ps[5][:, :], ones, B["cacc"][:, k, :], start=(k == 0), stop=(k == 3))
                mm.then_inc(sems("mean"), 1)
                norm_pe(E, **NORMS["ln"])
                E.meet()
                products("out", 8, h_hi, h_lo)
                E.meet()
                norm_pe(E, **NORMS["cross"])
                E.meet()
                products("cq", 8, h_hi, h_lo)
                for u in range(17):
                    if u == 0:
                        emptied(E, TILE["cq"] + 6)
                        emptied(E, TILE["cq"] + 7)
                    if u < 16:
                        h, i = u // TB, u % TB
                        E.at("probs", 32 + u - 1)
                        for b in range(2):
                            mm = nc.tensor.matmul(ps[2 + u % 2][:, 0:NMEM], B["qx"][:, 2 * h + b, i * P:(i + 1) * P],
                                                  B["kmem"][:, 2 * h + b, :], start=(b == 0), stop=(b == 1))
                        mm.then_inc(sems("scores"), 1)
                    if u >= 1:
                        w = u - 1
                        h, i = w // TB, w % TB
                        E.wait("att")
                        E.at("attT", 16 + w - 1)
                        for m in range(MB):
                            mm = turn(ps[4 + w % 2][:, m * P:(m + 1) * P], B["px"][:, w % 2, m * P:(m + 1) * P])
                        mm.then_inc(sems("att_turned"), 1)
                        if i == TB - 1:
                            E.at("attT", 16 + w + 1)
                            E.at("xo_taken", 2 * h)
                            for b in range(2):
                                for m in range(MB):
                                    mm = nc.tensor.matmul(ps[6 + b][:, :], B["vmem"][:, m, (2 * h + b) * P:(2 * h + b + 1) * P],
                                                          B["pxT"][:, h % 2, m, :], start=(m == 0), stop=(m == MB - 1))
                                mm.then_inc(sems("xo"), 1)
                E.meet()
                products("co", 8, h_hi, h_lo)
                E.meet()
                norm_pe(E, **NORMS["ffn"])
                E.meet()
                products("up", 44, h_hi, h_lo)
                E.meet()
                t0 = TILE["down"]
                for t in range(t0, t0 + 22):
                    pe.wait_ge(sems("weights_split"), t + 1)
                    for k in range(8):
                        d, f = divmod(8 * (t - t0) + k, FFB)
                        if f == 0 and d >= 2:
                            E.at("down_taken", d - 1)
                        mm = three(ps[3 + d % 2][:, :], None, B["zH"][:, f, :], B["zL"][:, f, :], k, t % 2, f == 0, f == FFB - 1)
                        if k == 7:
                            mm.then_inc(sems(f"tile_done{t % 2}"), 1)
                        elif f == FFB - 1:
                            mm.then_inc(sems("down"), 1)
                E.meet()
                norm_pe(E, **NORMS["final"])
                E.meet()
            if second:
                second_pe(E, products, one_tile, turn, h_hi, h_lo)

        @block.scalar
        def _(eng):
            E = side(eng, "act")
            eng.wait_ge(sems("consts_in"), 32)

            def copy_tiles(name, n, to, w=S, at=0, func=ACT.Copy):
                for b in range(n):
                    t = TILE[name] + at + b
                    tile_ready(E, t)
                    empties(act.activation(to(b), bank(t, w), func), t)

            if first:
                E.wait("lam_sums", 2)
                act.activation(sc[:, 2:4], sc[:, 0:2], ACT.Exp).then_inc(sems("lam_exp"), 1)
                eng.wait_ge(sems("mem_in"), 16)
                norm_act(E, **NORMS["mem"])
                E.meet()
                copy_tiles("ckv", 8, lambda b: B["kmem"][:, b, :], NMEM)
                for b in range(8):
                    if b >= 4:
                        E.at("mem_turn", b - 3)
                    t = TILE["ckv"] + 8 + b
                    tile_ready(E, t)
                    empties(act.activation(tmp[:, b % 4, 0:NMEM], bank(t, NMEM), ACT.Copy), t)
                E.meet()
                eng.dma_start(B["pos"][:], a["pos"].partition_broadcast(P)).then_inc(sems("pos_in"), 16)
                eng.wait_ge(sems("x_in"), 16)
                norm_act(E, **NORMS["mix"])
                E.meet()
                E.wait("angles")
                act.activation(B["sin"][:], B["att"][:, 0, :], ACT.Sin).then_inc(sems("sines"), 1)
                act.activation(B["cos"][:], B["att"][:, 0, :], ACT.Sin, scale=0.5).then_inc(sems("sines"), 1)
                for b in range(4):
                    t = TILE["in_u"] + 2 * b + 1
                    tile_ready(E, t)
                    empties(act.activation(tmp[:, b, :], bank(t), ACT.Sigmoid), t)
                copy_tiles("in_qkv", 8, lambda b: B["qkT"][:, b, :])
                copy_tiles("in_qkv", 4, lambda b: B["vT"][:, b, :], at=8)
                for b in range(4):
                    E.wait("v_turned")
                    act.activation(B["vtok"][:, :, b * P:(b + 1) * P],
                                            ps[5 + b % 2][:, :].rearrange("p (t d) -> p t d", t=TB), ACT.Copy).then_inc(sems("v_copied"), 1)
                E.meet()
                units = [(h, i) for h in range(4) for i in range(TB)]

                def probabilities(u):
                    w = P * (units[u][1] + 1)
                    E.at("att", u - 1)
                    for c in range(2):
                        E.wait("row_max")
                        act.activation(B["p"][:, u % 2, c, 0:w], ps[2 + 2 * (u % 2) + c][:, 0:w], ACT.Exp,
                                                bias=ss[:, u % 2, 2 + c:3 + c], scale=0.125,
                                                accum_out=ss[:, u % 2, 4 + c:5 + c]).then_inc(sems("probs"), 1)

                probabilities(0)
                for u, (h, i) in enumerate(units):
                    if u + 1 < len(units):
                        probabilities(u + 1)
                    E.wait("att_turned")
                    E.at("pv", u - 1)
                    act.activation(B["attT"][:, u % 2, 0:P * (i + 1)], ps[6][:, 0:P * (i + 1)], ACT.Copy).then_inc(sems("attT"), 1)
                    if i == TB - 1:
                        E.at("pv", u + 1)
                        act.activation(B["oT"][:, h, :], ps[7][:, :], ACT.Copy).then_inc(sems("oT"), 1)
                E.meet()
                norm_act(E, **NORMS["heads"])
                E.at("centred", 4)
                norm_act(E, **NORMS["ln"])
                for k in range(4):
                    if k == 0:
                        E.wait("ln_done")
                    act.activation(B["cacc"][:, k, :], B["cacc"][:, k, :], ACT.Silu, bias=PM("ln_b", k)).then_inc(sems("silu"), 1)
                for k in range(4):
                    E.at("silu", k + 1)
                    act.activation(hH[:, 4 + k, :], B["cacc"][:, k, :], ACT.Copy).then_inc(sems("hi_ready"), 1)
                E.meet()
                E.meet()
                norm_act(E, **NORMS["cross"])
                E.meet()
                copy_tiles("cq", 8, lambda b: B["qx"][:, b, :])
                for u in range(17):
                    if u < 16:
                        E.wait("row_max")
                        E.at("att_turned", 16 + u - 1)
                        act.activation(B["px"][:, u % 2, :], ps[2 + u % 2][:, 0:NMEM], ACT.Exp,
                                                bias=ss[:, u % 2, 2:3], scale=1.0 / 16,
                                                accum_out=ss[:, u % 2, 4:5]).then_inc(sems("probs"), 1)
                    if u >= 1:
                        w = u - 1
                        h, i = w // TB, w % TB
                        E.wait("att_turned")
                        E.at("xo", 2 * (h - 1))
                        act.activation(B["pxT"][:, h % 2, :, i * P:(i + 1) * P],
                                                ps[4 + w % 2][:, 0:NMEM].rearrange("p (m t) -> p m t", m=MB),
                                                ACT.Copy).then_inc(sems("attT"), 1)
                        if i == TB - 1:
                            for b in range(2):
                                E.wait("xo")
                                act.activation(hH[:, 2 * h + b, :], ps[6 + b][:, :], ACT.Copy).then_inc(sems("xo_hi"), 1)
                E.meet()
                E.meet()
                norm_act(E, **NORMS["ffn"])
                E.meet()
                for i in range(FFB + 2):
                    if i < FFB:
                        for c in range(2):
                            t = TILE["up"] + 2 * i + c
                            tile_ready(E, t)
                            E.at("ffn_conv", 2 * (i - 2) + c + 1)
                            empties(act.activation(B["uab"][:, i % 2, c, 2:S + 2], bank(t), ACT.Copy), t)
                    if 1 <= i <= FFB:
                        E.at("ffn_conv", 2 * (i - 1) + 2)
                        s = (i - 1) % 2
                        act.activation(sq[:, 2 * s, :], sq[:, 2 * s, :], ACT.Silu).then_inc(sems("ffn_silu"), 1)
                    if i >= 2:
                        hi_part(E, B["zH"][:, i - 2, :])
                E.meet()
                E.meet()
                norm_act(E, **NORMS["final"])
                E.meet()
            if second:
                second_act(E, eng, copy_tiles)
            eng.dma_start(a["out"].rearrange("(k p) t -> p k t", p=P), xT[:]).then_inc(sems("out_stored"), 16)
            eng.wait_ge(sems("out_stored"), 16)

        @block.vector
        def _(eng):
            E = side(eng, "dve")
            chain = Chain(eng, sems("dve_step"))
            eng.wait_ge(sems("consts_in"), 32)

            def add_tiles(name, n=8):
                for b in range(n):
                    t = TILE[name] + b
                    tile_ready(E, t)
                    empties(v.tensor_tensor(xT[:, b, :], xT[:, b, :], bank(t), ALU.add), t)

            if first:
                for n in range(2):
                    chain(v.tensor_tensor(tmp[:, n, 0:64], PM("lam", 128 * n, 64), PM("lam", 128 * n + 64, 64), ALU.mult))
                    v.tensor_reduce(sc[:, n:n + 1], tmp[:, n, 0:64], AX, ALU.add).then_inc(sems("lam_sums"), 1)
                chain(v.tensor_scalar(sc[:, 4:5], PM("subln"), 1.0 - 0.2, None, ALU.mult))
                E.wait("lam_exp")
                chain(v.tensor_scalar(sc[:, 6:7], sc[:, 3:4], sc[:, 2:3], -0.2, ALU.subtract, ALU.add))
                eng.wait_ge(sems("mem_in"), 16)
                norm_dve(E, chain, **NORMS["mem"])
                E.meet()
                for b in range(8):
                    E.wait("mem_turn")
                    v.tensor_copy(B["vmem"][:, :, b * P:(b + 1) * P],
                                           ps[5 + b % 2][:, 0:NMEM].rearrange("p (m d) -> p m d", m=MB)).then_inc(sems("mem_turned"), 1)
                E.meet()
                eng.wait_ge(sems("x_in"), 16)
                norm_dve(E, chain, **NORMS["mix"])
                E.meet()
                ang, y = B["att"][:, 0, :], B["att"][:, 1, :]
                eng.wait_ge(sems("pos_in"), 16)
                chain(v.tensor_copy(B["attT"][:, 0, :], B["pos"][:]))
                chain(v.tensor_scalar(ang, B["attT"][:, 0, :], C("invfreq"), None, ALU.mult))
                magic = 1.5 * 2.0 ** 23
                chain(v.tensor_scalar(y, ang, 1.0 / (2 * math.pi), magic, ALU.mult, ALU.add))
                chain(v.tensor_scalar(y, y, -magic, None, ALU.add))
                c1 = 6.28125
                c2 = float(np.float32(np.floor((2 * math.pi - c1) * 2 ** 21) / 2 ** 21))
                for c in (c1, c2, 2 * math.pi - c1 - c2):
                    chain(v.scalar_tensor_tensor(out=ang, in0=y, scalar=-c, in1=ang, op0=ALU.mult, op1=ALU.add))
                v.tensor_scalar(ang, ang, 3.1415925, -3.1415925, ALU.min, ALU.max).then_inc(sems("angles"), 1)
                E.wait("sines", 2)
                chain(v.tensor_tensor(B["cos"][:], B["cos"][:], B["cos"][:], ALU.mult))
                chain(v.tensor_scalar(B["cos"][:], B["cos"][:], -2.0, 1.0, ALU.mult, ALU.add))
                chain(v.memset(B["cpad"][:, :, 0:TAPS - 1], 0.0))
                for b in range(4):
                    t = TILE["in_u"] + 2 * b
                    tile_ready(E, t)
                    emptied(E, t + 1)
                    empties(v.tensor_tensor(B["cpad"][:, b, TAPS - 1:TAPS - 1 + S], bank(t), tmp[:, b, :], ALU.mult), t)
                for k in range(TAPS):
                    for b in range(4):
                        w = PM("cv_w", b * TAPS + k)
                        x = B["cpad"][:, b, k:k + S]
                        if k == 0:
                            emptied(E, TILE["in_u"] + 2 * b)
                            ins = v.tensor_scalar(B["cacc"][:, b, :], x, w, PM("cv_b", b), ALU.mult, ALU.add)
                        else:
                            E.at("tap", 4 * k + b - 3)
                            ins = v.scalar_tensor_tensor(out=B["cacc"][:, b, :], in0=x, scalar=w,
                                                         in1=B["cacc"][:, b, :], op0=ALU.mult, op1=ALU.add)
                        ins.then_inc(sems("tap"), 1)
                for b in range(8):
                    q = B["qkT"][:, b, :]
                    E.wait("swapped")
                    chain(v.tensor_tensor(tmp[:, b % 2, :], ps[3 + b % 2][:, :], B["sin"][:], ALU.mult))
                    chain(v.tensor_tensor(q, q, B["cos"][:], ALU.mult))
                    v.tensor_tensor(q, q, tmp[:, b % 2, :], ALU.add).then_inc(sems("roped"), 1)
                E.meet()
                units = [(h, i) for h in range(4) for i in range(TB)]

                def maxima(u):
                    i = units[u][1]
                    for c in range(2):
                        b = ps[2 + 2 * (u % 2) + c]
                        E.wait("scores")
                        chain(v.tensor_tensor(b[:, i * P:(i + 1) * P], b[:, i * P:(i + 1) * P], C("causal"), ALU.add))
                        chain(v.tensor_reduce(ss[:, u % 2, c:c + 1], b[:, 0:P * (i + 1)], AX, ALU.max))
                        v.tensor_scalar(ss[:, u % 2, 2 + c:3 + c], ss[:, u % 2, c:c + 1], -0.125, None, ALU.mult).then_inc(sems("row_max"), 1)

                maxima(0)
                for u, (h, i) in enumerate(units):
                    if u + 1 < len(units):
                        maxima(u + 1)
                    w = P * (i + 1)
                    o = u % 2
                    E.wait("probs", 2)
                    chain(v.reciprocal(ss[:, o, 6:8], ss[:, o, 4:6]))
                    chain(v.tensor_tensor(ss[:, o, 8:9], ss[:, o, 7:8], sc[:, 6:7], ALU.mult))
                    E.at("att_turned", u - 1)
                    chain(v.tensor_scalar(B["att"][:, o, 0:w], B["p"][:, o, 0, 0:w], ss[:, o, 6:7], None, ALU.mult))
                    v.scalar_tensor_tensor(out=B["att"][:, o, 0:w], in0=B["p"][:, o, 1, 0:w], scalar=ss[:, o, 8:9],
                                                    in1=B["att"][:, o, 0:w], op0=ALU.mult, op1=ALU.add).then_inc(sems("att"), 1)
                E.meet()
                norm_dve(E, chain, **NORMS["heads"])
                E.wait("mean")
                for k in range(4):
                    v.scalar_tensor_tensor(out=B["cacc"][:, k, :], in0=ps[5][:, :], scalar=-1.0 / 512,
                                                    in1=B["cacc"][:, k, :], op0=ALU.mult, op1=ALU.add).then_inc(sems("centred"), 1)
                E.at("centred", 4)
                norm_dve(E, chain, **NORMS["ln"])
                E.at("rb_used", 1 + 1 + 4 + 1)
                v.tensor_scalar(sc[:, 9:10], sc[:, 4:5], 1.0, None, ALU.mult).then_inc(sems("ln_done"), 1)
                for k in range(4):
                    E.wait("hi_ready")
                    v.tensor_tensor(hL[:, 4 + k, :], B["cacc"][:, k, :], hH[:, 4 + k, :].bitcast(F32), ALU.subtract).then_inc(sems("lo_ready"), 1)
                E.meet()
                add_tiles("out")
                E.meet()
                norm_dve(E, chain, **NORMS["cross"])
                E.meet()
                for u in range(17):
                    if u < 16:
                        E.wait("scores")
                        chain(v.tensor_reduce(ss[:, u % 2, 0:1], ps[2 + u % 2][:, 0:NMEM], AX, ALU.max))
                        v.tensor_scalar(ss[:, u % 2, 2:3], ss[:, u % 2, 0:1], -1.0 / 16, None, ALU.mult).then_inc(sems("row_max"), 1)
                    if u >= 1:
                        o = (u - 1) % 2
                        E.wait("probs")
                        chain(v.reciprocal(ss[:, o, 6:7], ss[:, o, 4:5]))
                        v.tensor_scalar(B["px"][:, o, :], B["px"][:, o, :], ss[:, o, 6:7], None, ALU.mult).then_inc(sems("att"), 1)
                        if u % TB == 0:
                            h = (u - 1) // TB
                            for b in range(2):
                                E.wait("xo_hi")
                                v.tensor_tensor(hL[:, 2 * h + b, :], ps[6 + b][:, :], hH[:, 2 * h + b, :].bitcast(F32),
                                                         ALU.subtract).then_inc(sems("xo_taken"), 1)
                E.meet()
                add_tiles("co")
                E.meet()
                norm_dve(E, chain, **NORMS["ffn"])
                chain(v.memset(B["uab"][:, :, :, 0:2], 0.0))
                E.meet()
                held = []
                for i in range(FFB + 2):
                    if i < FFB:
                        E.at("v_ready", E.n["made v"])
                        for c in range(2):
                            t = TILE["up"] + 2 * i + c
                            emptied(E, t)
                            u = B["uab"][:, i % 2, c, :]
                            to = sq[:, 2 * (i % 2) + c, :]
                            wcol = 3 * (i + c * FFB)
                            chain(v.tensor_scalar(to, u[:, 2:S + 2], PM("ffn_w", wcol + 2), None, ALU.mult))
                            for k in (1, 0):
                                ins = v.scalar_tensor_tensor(out=to, in0=u[:, k:S + k], scalar=PM("ffn_w", wcol + k), in1=to,
                                                             op0=ALU.mult, op1=ALU.add)
                                if k:
                                    chain(ins)
                            ins.then_inc(sems("ffn_conv"), 1)
                    if 1 <= i <= FFB:
                        E.wait("ffn_silu")
                        s = (i - 1) % 2
                        n = E.made("v")
                        E.at("ffn_conv", 2 * i)
                        v.tensor_tensor(tmp[:, n % 4, :], sq[:, 2 * s, :], sq[:, 2 * s + 1, :], ALU.mult).then_inc(sems("v_ready"), 1)
                        held.append((n, (B["zH"][:, i - 1, :], B["zL"][:, i - 1, :])))
                    if i >= 2:
                        lo_part(E, held.pop(0))
                E.meet()
                for d in range(8):
                    if d % 4 == 3:
                        tile_ready(E, TILE["down"] + (22 * (d + 1)) // 8 - 1)
                    else:
                        E.wait("down")
                    v.tensor_tensor(xT[:, d, :], xT[:, d, :], ps[3 + d % 2][:, :], ALU.add).then_inc(sems("down_taken"), 1)
                E.meet()
                norm_dve(E, chain, **NORMS["final"])
                E.meet()
            if second:
                second_dve(E, eng, chain, add_tiles)


def pack(w):
    k, m = w.shape
    return w.reshape(k // P, P, m // P, P).transpose(2, 1, 0, 3).reshape(m // P, P, k)


def columns(v, n):
    return np.asarray(v).reshape(n, P).T


def first_weights(i):
    w_in, ckv, up, down = i["w_in"][0], i["w_ckv"][0], i["w_up"][0], i["w_down"][0]
    u = pack(w_in[:, 1536:])
    ups = pack(up)
    pairs = lambda t, n: np.stack([t[:n], t[n:]], 1).reshape(2 * n, P, D)
    downs = down.reshape(FFB, P, 8, P).transpose(2, 0, 1, 3).reshape(22, 8, P, P).transpose(0, 2, 1, 3).reshape(22, P, D)
    return [pack(ckv), pairs(u, 4), pack(w_in[:, :1536]), pack(i["w_out"][0]), pack(i["w_cq"][0]),
            pack(i["w_co"][0]), pairs(ups, FFB), downs]


def parameters(i):
    one = lambda v, n: columns(v, n)
    taps = lambda w, n: np.asarray(w).reshape(w.shape[0], n, P).transpose(2, 1, 0).reshape(P, -1)
    rows = lambda v: np.broadcast_to(np.asarray(v).reshape(1, -1), (P, np.asarray(v).size))
    got = [one(i["norm_mix_g"], 8), one(i["norm_cross_g"], 8), one(i["norm_mem_g"], 8), one(i["norm_ffn_g"], 8),
           one(i["norm_final_g"], 8), one(i["mix_norm_w_2"], 8), one(i["ffn_norm_w_2"], 8), one(i["subln_g"], 1),
           taps(i["cv_dw_w"][0], 4), one(i["cv_dw_b"], 4), one(i["cv_ln_g"], 4), one(i["cv_ln_b"], 4),
           taps(i["ffn_dw_w"][0], 44), one(i["sb_q_norm_w_2"], 1), one(i["sb_k_norm_w_2"], 1),
           taps(i["gdn_conv_w_2"][0], 24), one(i["gdn_out_norm_w_2"], 1),
           rows(i["lam_q1"]), rows(i["lam_k1"]), rows(i["lam_q2"]), rows(i["lam_k2"]),
           rows(i["gdn_a_log_2"]), rows(i["gdn_dt_bias_2"])]
    return np.concatenate(got, 1)


def second_weights(i):
    w = i["w_in_2"][0]
    ba = np.concatenate([w[:, 7168:7184], np.zeros((D, P - 16), w.dtype)], 1)
    u = i["peer_u_2"][0].reshape(GROUPS, 8, P, KB, P).transpose(0, 1, 4, 3, 2).reshape(GROUPS, 8, P, D)
    d = i["peer_v_2"][0].reshape(GROUPS, 8, P, KB, P).transpose(0, 3, 2, 1, 4).reshape(GROUPS, 8, P, D)
    return [pack(w[:, :3072]), pack(w[:, 7184:8208]), pack(i["w_branch_sb_2"][0]), pack(w[:, 3072:6144]), pack(ba),
            pack(w[:, 6144:7168]), pack(w[:, 8208:9232]), pack(i["w_branch_gdn_2"][0]), pack(i["w_out_2"][0]),
            pack(i["peer_w_q_2"][0]), np.concatenate([u, d], 1).reshape(16 * GROUPS, P, D)]


def laid_out(i):
    keys = np.stack([i["peer_keys1_2"][0], i["peer_keys2_2"][0]], 1)
    return {
        "weights": np.concatenate(first_weights(i) + second_weights(i)),
        "consts": constants(),
        "params": np.ascontiguousarray(parameters(i)),
        "xT": np.ascontiguousarray(i["x"][0].T),
        "memT": np.ascontiguousarray(i["mem"][0].T),
        "pos": np.ascontiguousarray(i["positions"][0]),
        "keys": np.ascontiguousarray(keys.transpose(0, 1, 3, 2).reshape(2 * NH2, P, P)),
    }


def kernel(**inputs):
    import concourse.bacc as bacc
    from concourse.bass_utils import run_bass_kernel_spmd

    arrays = laid_out({k: np.asarray(v) for k, v in inputs.items()})
    nc = bacc.Bacc("TRN2", target_bir_lowering=False, num_devices=1)
    a = {k: nc.dram_tensor(f"in_{k}", v.shape, mybir.dt.from_np(v.dtype), kind="ExternalInput").ap()
         for k, v in arrays.items()}
    a["out"] = nc.dram_tensor("out_xT", (D, S), F32, kind="ExternalOutput").ap()
    a["gates"] = nc.dram_tensor("gates", (TG, P, P, 32), F32, kind="Internal").ap()
    build(nc, a)
    r = run_bass_kernel_spmd(nc, [{f"in_{k}": v for k, v in arrays.items()}], core_ids=[0])
    return np.ascontiguousarray(r.results[0]["out_xT"].T)[None]
```

```python
import math
from contextlib import ExitStack

import numpy as np

import concourse.bass as bass
from concourse import mybir

P = 128
F32 = mybir.dt.float32
F32R = mybir.dt.float32r
U32 = mybir.dt.uint32
I32 = mybir.dt.int32
ALU = mybir.AluOpType
ACT = mybir.ActivationFunctionType
AX = mybir.AxisListType.X

D = 1024
S = 512
KB = D // P
TB = S // P
NMEM = 256
MB = NMEM // P
EPS = 1e-6
TAPS = 31
FFB = 2816 // P
NH2 = 8
GROUPS = 16
EARLY = 10
LATE = GROUPS - EARLY
TG = S // 32
NEG = -1e30

CONSTS = {}
_at = 0
for _name, _n in (("ident", P), ("ones", P), ("swap", P), ("causal", P), ("low", P), ("ups", P), ("upi", P),
                  ("levels", 7 * P), ("iota", P), ("invfreq", 1)):
    CONSTS[_name] = (_at, _n)
    _at += _n
N_CONST = _at

PARAMS = {}
_at = 0
for _name, _n in (("norm_mix", 8), ("norm_cross", 8), ("norm_mem", 8), ("norm_ffn", 8), ("norm_final", 8),
                  ("mix2", 8), ("ffn2", 8), ("subln", 1), ("cv_w", 4 * TAPS), ("cv_b", 4), ("ln_g", 4),
                  ("ln_b", 4), ("ffn_w", 44 * 3), ("sbq", 1), ("sbk", 1), ("gdn_w", 24 * 4), ("gdn_g", 1),
                  ("lam", 4 * 64), ("a_log", 8), ("dt", 8)):
    PARAMS[_name] = (_at, _n)
    _at += _n
N_PARAM = _at

TILE = {}
_at = 0
for _name, _n in (("ckv", 16), ("in_u", 8), ("in_qkv", 12), ("out", 8), ("cq", 8), ("co", 8), ("up", 44),
                  ("down", 22), ("sb_qkv", 24), ("gate_sb", 8), ("branch_sb", 8), ("ba", 1), ("gdn_qkv", 24),
                  ("z", 8), ("gate_gdn", 8), ("branch_gdn", 8), ("out2", 8), ("wq", 16), ("peer", 16 * GROUPS)):
    TILE[_name] = _at
    _at += _n
N_TILES = _at


def constants():
    c = np.zeros((P, N_CONST), np.float32)
    r = np.arange(P)

    def put(name, a):
        o, n = CONSTS[name]
        c[:, o:o + n] = a

    put("ident", np.eye(P))
    put("ones", 1.0)
    swap = np.zeros((P, P))
    for half in range(2):
        for i in range(8):
            swap[64 * half + i + 8, 64 * half + i] = -1.0
            swap[64 * half + i, 64 * half + i + 8] = 1.0
    put("swap", swap)
    put("causal", np.where(r[None, :] <= r[:, None], 0.0, NEG))
    put("low", r[:, None] > r[None, :])
    put("ups", r[:, None] < r[None, :])
    put("upi", r[:, None] <= r[None, :])
    levels = np.zeros((P, 7, P))
    for n in range(7):
        b = 1 << n
        same = r[:, None] // (2 * b) == r[None, :] // (2 * b)
        levels[:, n, :] = same & (r[:, None] // b % 2 == 0) & (r[None, :] // b % 2 == 1)
    put("levels", levels.reshape(P, -1))
    put("iota", r[None, :])
    freq = np.float32(500000.0) ** (-np.arange(0, 16, 2, dtype=np.float32) / np.float32(16))
    col = np.zeros(P)
    for half in range(2):
        col[64 * half:64 * half + 8] = freq
        col[64 * half + 8:64 * half + 16] = freq
    put("invfreq", col[:, None])
    return c


class Chain:

    def __init__(self, eng, sem):
        self.eng, self.sem, self.n = eng, sem, 0

    def __call__(self, ins):
        ins.then_inc(self.sem, 1)
        self.n = self.n + 1
        self.eng.wait_ge(self.sem, self.n)


class Side:

    def __init__(self, eng, sems, barrier_name, others):
        self.eng, self.sems = eng, sems
        self.n = {}
        self.phase, self.me, self.others = 0, barrier_name, others

    def wait(self, name, k=1):
        self.n[name] = self.n.get(name, 0) + k
        self.eng.wait_ge(self.sems(name), self.n[name])

    def at(self, name, value):
        if value > 0:
            self.eng.wait_ge(self.sems(name), value)

    def made(self, name):
        k = self.n.get("made " + name, 0)
        self.n["made " + name] = k + 1
        return k

    def prime(self, name, k=1):
        self.eng.drain().then_inc(self.sems(name), k)

    def arrive(self):
        self.phase += 1
        self.eng.drain().then_inc(self.sems(self.me), 1)

    def meet(self):
        self.arrive()
        for o in self.others:
            self.eng.wait_ge(self.sems(o), self.phase)


def build(nc, a, first=True, second=True):
    with ExitStack() as ctx:
        sem_of = {}

        def sems(name):
            if name not in sem_of:
                sem_of[name] = ctx.enter_context(nc.semaphore(name))
            return sem_of[name]

        def sb(name, shape, dt=F32, on=None):
            return (on or ctx).enter_context(nc.sbuf_tensor("sb_" + name, shape, dt))

        ps = [ctx.enter_context(nc.psum_tensor(f"bank{i}", [P, 512], F32)) for i in range(8)]

        cst = sb("consts", [P, N_CONST])
        par = sb("params", [P, N_PARAM])
        xT = sb("xT", [P, KB, S])
        hH = sb("hH", [P, KB, S], F32R)
        hL = sb("hL", [P, KB, S], F32R)
        raw = sb("raw", [P, 4, D])
        wH = sb("wH", [P, 2, D], F32R)
        wL = sb("wL", [P, 2, D], F32R)
        sq = sb("sq", [P, 4, S])
        tmp = sb("tmp", [P, 4, S])
        dg = sb("dg", [P, 2, S])
        st = sb("st", [P, 5, 64])

        def C(name, i=0, n=None):
            o, w = CONSTS[name]
            return cst[:, o + i:o + i + (n or w)]

        def PM(name, i=0, n=1):
            return par[:, PARAMS[name][0] + i:PARAMS[name][0] + i + n]

        ss = sb("ss", [P, 2, 16])
        cell = sb("cell", [P, 2])
        sc = sb("sc", [P, 16])

        def over(spec, inner=()):
            with ExitStack() as e:
                got = {n: sb(n, s, d, on=e) for n, s, d in spec}
                for more in inner:
                    got.update(more())
            return got

        B = {}
        B.update(over([("kmem", [P, 8, NMEM], F32), ("vmem", [P, MB, D], F32)], (
            lambda: over([("memT", [P, 8, NMEM], F32), ("mH", [P, 8, NMEM], F32R), ("mL", [P, 8, NMEM], F32R),
                          ("vmT", [P, 4, NMEM], F32)]),
            lambda: over([("qkT", [P, 8, S], F32), ("vT", [P, 4, S], F32), ("vtok", [P, TB, S], F32),
                          ("cpad", [P, 4, S + 32], F32), ("cacc", [P, 4, S], F32), ("cos", [P, S], F32),
                          ("sin", [P, S], F32), ("pos", [P, S], I32), ("p", [P, 2, 2, S], F32),
                          ("att", [P, 2, S], F32), ("attT", [P, 2, S], F32), ("oT", [P, 4, S], F32)]),
            lambda: over([("qx", [P, 8, S], F32), ("px", [P, 2, NMEM], F32), ("pxT", [P, 2, MB, S], F32)]))))
        B.update(over([("zH", [P, FFB, S], F32R), ("zL", [P, FFB, S], F32R), ("uab", [P, 2, 2, S + 2], F32)]))
        B.update(over([("merged", [P, 8, S], F32)], (
            lambda: over([("sbq", [P, 8, S], F32)], (
                lambda: over([("sbk", [P, 8, S], F32), ("sbv", [P, 8, S], F32), ("sbvt", [P, TB, D], F32),
                              ("sbt", [P, 2, 1280], F32), ("Lp", [P, 1280], F32)]),
                lambda: over([("oH", [P, 8, S], F32R), ("oL", [P, 8, S], F32R)]))),
            lambda: over([("gq", [P, 8, S], F32)], (
                lambda: over([("gk", [P, 8, S], F32), ("gv", [P, 8, S], F32)], (
                    lambda: over([("gpad", [P, 4, S + 4], F32)]),
                    lambda: over([(f"gd{i}", [P, 4, P], F32) for i in range(10)] + [
                        ("state", [P, 8, P], F32), ("ga", [P, 10, TB, 8], F32)]))),
                lambda: over([("goH", [P, 8, S], F32R), ("goL", [P, 8, S], F32R), ("gg", [P, 8, S], F32)]))))))
        B.update(over([("slots", [P, 3, S], F32)], (
            lambda: over([("qp", [P, 16, S], F32), ("keys", [P, 16, P], F32), ("work", [P, 256], F32),
                          ("cand", [P, 256], F32), ("v12", [P, 2, 16], F32), ("i12", [P, 8, 2, 16], U32),
                          ("cv", [P, 8, 16], F32), ("ci", [P, 8, 16], U32), ("cc", [P, 2, 8, 16], U32),
                          ("cf", [P, 2, 8, 16], F32), ("if12", [P, 8, 2, 16], F32), ("eq", [P, 2048], F32),
                          ("eg", [P, 4, P], F32)]),
            lambda: over([("onehot", [P, 4, 4, P], F32), ("gated", [P, 4, 4, P], F32),
                          ("stage", [P, 2, P, 32], F32)]))))
        B.update(over([("Gt", [P, TG, 8, 32], F32), ("Ga", [P, 8, S], F32), ("pzH", [P, 2, 8, S], F32R),
                       ("pzL", [P, 2, 8, S], F32R)]))

        gates, acts = a["gates"], a["acts"]
        block = ctx.enter_context(nc.Block())
        n_loop = N_TILES // 4 * 4
        W = a["weights"]
        Wl = W[0:n_loop].rearrange("(j s) p f -> j s p f", s=4)

        ident, ones = C("ident"), C("ones")

        def freed(t):
            past = min(max(t - TILE["down"], 0), 22)
            return t // 2 - past // 2

        def tile_ready(E, t, j=None, per=0):
            E.eng.wait_ge(sems(f"tile_done{t % 2}"), t // 2 + 1 if j is None else t // 2 + 1 + per * j)

        def emptied(E, t, j=None, per=0):
            v = freed(t) + 1
            E.eng.wait_ge(sems(f"bank_free{t % 2}"), v if j is None else v + per * j)

        def empties(ins, t):
            ins.then_inc(sems(f"bank_free{t % 2}"), 1)

        def bank(t, w=S):
            return ps[t % 2][:, 0:w]


        def square(E, x, w=S):
            i = E.made("sq")
            E.at("sq_used", i - 3)
            nc.scalar.activation(sq[:, i % 4, 0:w], x, ACT.Square).then_inc(sems("sq_ready"), 1)

        def norm_act(E, groups, nk, src, nt=TB, split=False, squared=False, when=None, **_):
            w = nt * P
            for g in range(0 if squared else groups):
                for k in range(nk):
                    if when:
                        when(k)
                    square(E, src(g, k), w)
            root_act(E, groups * nt)
            if split:
                for g in range(groups):
                    for k in range(nk):
                        hi_part(E, split(g, k)[0], w)

        def root_act(E, m):
            E.wait("var_ready")
            nc.scalar.activation(st[:, 1, 0:m], st[:, 0, 0:m], ACT.Sqrt).then_inc(sems("std_ready"), 1)

        def sum_block(E, first, g=0, nt=TB):
            if first:
                E.at("var_ready", E.made("norm"))
            E.wait("sq_ready")
            i = E.made("sq")
            for t in range(nt):
                o = g * nt + t
                mm = nc.tensor.matmul(ps[2][:, o:o + 1], sq[:, i % 4, t * P:(t + 1) * P], ones[:, 0:1],
                                      start=(first and t == 0), stop=True, skip_group_check=True)
            mm.then_inc(sems("sq_used"), 1)

        def norm_pe(E, groups, nk, src, nt=TB, summed=False, **_):
            w = nt * P
            for g in range(0 if summed else groups):
                for k in range(nk):
                    sum_block(E, g == 0 and k == 0, g, nt)
            for g in range(groups):
                spread_pe(E, w)

        def spread_pe(E, w=S):
            i = E.made("rb")
            E.wait("diag_ready")
            E.at("rb_used", i - 1)
            nc.tensor.matmul(ps[3 + i % 2][:, 0:w], ones, dg[:, i % 2, 0:w],
                             start=True, stop=True).then_inc(sems("rb_ready"), 1)

        def norm_dve(E, chain, groups, nk, src, gain, scale, nt=TB, split=None, dst=None, each="lo_ready"):
            w = nt * P
            root_dve(E, chain, groups, nk, scale, nt)
            diagonal(E, 0, nt)
            held = []
            for g in range(groups):
                if g + 1 < groups:
                    diagonal(E, g + 1, nt)
                spread_out(E, g, nk, src, gain, w, split, dst, each, held)

        def root_dve(E, chain, groups, nk, scale, nt=TB):
            m = groups * nt
            v = nc.vector
            E.wait("sq_used", groups * nk)
            v.tensor_scalar(st[:, 0, 0:m], ps[2][:, 0:m], scale, EPS, ALU.mult, ALU.add).then_inc(sems("var_ready"), 1)
            E.wait("std_ready")
            chain(v.reciprocal(st[:, 2, 0:m], st[:, 1, 0:m]))
            chain(v.tensor_tensor(st[:, 3, 0:m], st[:, 2, 0:m], st[:, 2, 0:m], ALU.mult))
            chain(v.tensor_tensor(st[:, 3, 0:m], st[:, 3, 0:m], st[:, 0, 0:m], ALU.mult))
            chain(v.tensor_scalar(st[:, 3, 0:m], st[:, 3, 0:m], -0.5, 1.5, ALU.mult, ALU.add))
            chain(v.tensor_tensor(st[:, 4, 0:m], st[:, 2, 0:m], st[:, 3, 0:m], ALU.mult))

        def diagonal(E, g, nt=TB):
            i = E.made("diag")
            E.at("rb_ready", i - 1)
            nc.vector.tensor_tensor(dg[:, i % 2, 0:nt * P].rearrange("p (a b) -> p a b", b=P),
                                    ident.unsqueeze(1).to_broadcast([P, nt, P]),
                                    st[:, 4, g * nt:(g + 1) * nt].unsqueeze(2).to_broadcast([P, nt, P]),
                                    ALU.mult).then_inc(sems("diag_ready"), 1)

        def spread_out(E, g, nk, src, gain, w, split, dst, each, held):
            v = nc.vector
            E.wait("rb_ready")
            r = ps[3 + E.made("rbr") % 2][:, 0:w]
            for k in range(nk):
                to = dst(g, k) if dst else None
                if split:
                    if len(held) > 1:
                        lo_part(E, held.pop(0), w, each)
                    i = E.made("v")
                    to = tmp[:, i % 4, 0:w]
                    held.append((i, split(g, k)))
                gn = gain(g, k)
                if gn is None:
                    ins = v.tensor_tensor(to, src(g, k), r, ALU.mult)
                else:
                    ins = v.scalar_tensor_tensor(out=to, in0=src(g, k), scalar=gn, in1=r,
                                                 op0=ALU.mult, op1=ALU.mult)
                if split:
                    ins.then_inc(sems("v_ready"), 1)
                else:
                    ins.then_inc(sems("rb_used" if k == nk - 1 else each), 1)
            if split:
                while held:
                    lo_part(E, held.pop(0), w, "rb_used" if len(held) == 0 else each)

        def norm_beside_pe(E, b, k):
            for n in (2 * (b % 4), 2 * (b % 4) + 1) if k == 6 else ():
                if b < 4:
                    sum_block(E, n == 0, n)
                else:
                    spread_pe(E)

        def norm_beside_act(E, b, src):
            for g in (2 * b, 2 * b + 1) if b < 4 else ():
                square(E, src(g, 0))

        def norm_beside_dve(E, chain, b, groups, nk, src, gain, scale, dst):
            if b == 4:
                root_dve(E, chain, groups, nk, scale)
                diagonal(E, 0)
            for g in (2 * b - 8, 2 * b - 7) if b >= 4 else ():
                if g + 1 < groups:
                    diagonal(E, g + 1)
                spread_out(E, g, nk, src, gain, S, None, dst, None, None)

        def hi_part(E, H, w=S):
            E.wait("v_ready")
            i = E.made("v")
            nc.scalar.activation(H, tmp[:, i % 4, 0:w], ACT.Copy).then_inc(sems("hi_ready"), 1)

        def lo_part(E, what, w=S, name="lo_ready"):
            i, (H, L) = what
            E.wait("hi_ready")
            nc.vector.tensor_tensor(L, tmp[:, i % 4, 0:w], H.bitcast(F32), ALU.subtract).then_inc(sems(name), 1)

        HS = lambda g, k: (hH[:, k, :], hL[:, k, :])
        X = lambda g, k: xT[:, k, :]

        def main_norm(name):
            return dict(groups=1, nk=KB, src=X, gain=lambda g, k: PM(name, k), scale=1.0 / D, split=HS, each="h_ready")

        def beside(name, gain, scale):
            at = lambda g, k: B[name][:, g, :]
            return dict(groups=8, nk=1, src=at, dst=at, gain=gain, scale=scale)

        NORMS = {
            "mem": dict(groups=1, nk=KB, nt=MB, src=lambda g, k: B["memT"][:, k, :],
                        gain=lambda g, k: PM("norm_mem", k), scale=1.0 / D,
                        split=lambda g, k: (B["mH"][:, k, :], B["mL"][:, k, :]), each="h_ready"),
            "mix": main_norm("norm_mix"), "cross": main_norm("norm_cross"), "ffn": main_norm("norm_ffn"),
            "final": dict(groups=1, nk=KB, src=X, gain=lambda g, k: PM("norm_final", k), scale=1.0 / D, dst=X,
                          each="x_normed"),
            "mix2": main_norm("mix2"), "ffn2": main_norm("ffn2"),
            "heads": dict(groups=4, nk=1, src=lambda g, k: B["oT"][:, g, :], gain=lambda g, k: sc[:, 4:5],
                          scale=1.0 / P, split=lambda g, k: (hH[:, g, :], hL[:, g, :])),
            "ln": dict(groups=1, nk=4, src=lambda g, k: B["cacc"][:, k, :], gain=lambda g, k: PM("ln_g", k),
                       scale=1.0 / 512, dst=lambda g, k: B["cacc"][:, k, :]),
            "sb_q": beside("sbq", lambda g, k: sc[:, 5:6], 1.0 / P),
            "sb_k": beside("sbk", lambda g, k: PM("sbk"), 1.0 / P),
            "l2_q": beside("gq", lambda g, k: P ** -0.5, 1.0),
            "l2_k": beside("gk", lambda g, k: None, 1.0),
            "gdn": beside("gq", lambda g, k: PM("gdn_g"), 1.0 / P),
        }

        v = nc.vector
        act = nc.scalar

        offs = [0, 512, 896, 1152]
        qw = [S - P * kb for kb in range(TB)]

        sb_t = [B["sbt"][:, c, :] for c in range(2)]
        sb_a = [b[:].rearrange("p s t -> p (s t)")[:, 0:1280] for b in (sq, tmp)]

        G = [{}, {}]
        places = [B[f"gd{n}"][:] for n in range(10)] + [b[:, n, :].rearrange("p (x t) -> p x t", x=4)
                                                        for b in (sq, tmp) for n in range(4)]
        for n, name in enumerate(("kw", "vb", "er", "X", "LT", "aT", "T", "R", "N")):
            for c in range(2):
                G[c][name] = places[2 * n + c]
        LEVELS = 7
        X_BANK, Y_BANK = (6, 4), (7, 5)
        col = lambda x: slice(x * P, (x + 1) * P)

        def second_pe(E, products, products_and_sums, parts_ready, one_tile, turn, h_hi, h_lo):
            pe = E.eng
            norm_pe(E, **NORMS["mix2"])
            E.arrive()
            products("sb_qkv", 8, h_hi, h_lo, ready=parts_ready)

            def tiles_beside_norm(name, at=0, after=None):
                for b in range(8):
                    one_tile(TILE[name] + at + b, h_hi, h_lo, ready=lambda k: norm_beside_pe(E, b, k))
                    if after and b:
                        after(b - 1)
                if after:
                    after(7)

            def turn_values(b):
                emptied(E, TILE["sb_qkv"] + 16 + b)
                E.at("sbv_turned", b - 1)
                for t in range(TB):
                    mm = turn(ps[5 + b % 2][:, t * P:(t + 1) * P], B["sbv"][:, b, t * P:(t + 1) * P])
                mm.then_inc(sems("sbv_turn"), 1)

            tiles_beside_norm("sb_qkv", 8)
            tiles_beside_norm("sb_qkv", 16, turn_values)
            E.arrive()
            E.at("rb_used", E.n["made rb"])
            E.at("sbv_turned", 8)
            def sb_scores(h, kb):
                E.at("sb_L", TB * h - kb)
                E.at("sb_ls", TB * h - kb)
                nc.tensor.matmul(ps[4 + kb][:, 0:qw[kb]], B["sbk"][:, h, kb * P:(kb + 1) * P],
                                 B["sbq"][:, h, kb * P:S], start=True, stop=True).then_inc(sems("sb_z"), 1)

            def sb_sums(h, kb):
                E.at("sb_L", TB * h + TB - kb)
                E.at("sb_la", TB * h - kb)
                if kb == TB - 1:
                    E.at("sb_o_copied", h - 1)
                mm = nc.tensor.matmul(ps[kb][:, 0:qw[kb]], C("low"), B["Lp"][:, offs[kb]:offs[kb] + qw[kb]],
                                      start=True, stop=True)
                for later in range(kb + 1, TB):
                    mm = nc.tensor.matmul(ps[kb][:, P * (later - kb):qw[kb]], ones,
                                          B["Lp"][:, offs[later]:offs[later] + qw[later]],
                                          start=False, stop=True, skip_group_check=True)
                mm.then_inc(sems("sb_S"), 1)

            for kb in reversed(range(TB)):
                sb_scores(0, kb)
            for h in range(NH2 + 1):
                for kb in reversed(range(TB)):
                    if h + 1 < NH2:
                        sb_scores(h + 1, kb)
                    if h < NH2:
                        sb_sums(h, kb)
                if h >= 1:
                    E.at("sb_la", min(TB * h + 1, TB * NH2))
                    E.at("sb_am", TB * h)
                    for kb in range(TB):
                        mm = nc.tensor.matmul(ps[3][:, P * kb:S], B["sbvt"][:, kb, (h - 1) * P:h * P],
                                              sb_a[(h - 1) % 2][:, offs[kb]:offs[kb] + qw[kb]], start=(kb == 0), stop=True,
                                              skip_group_check=True)
                    mm.then_inc(sems("sb_o"), 1)
            E.arrive()
            E.arrive()
            products("gate_sb", 8, h_hi, h_lo)
            E.wait("sb_o_parts", 8)
            products("branch_sb", 8, lambda k: B["oH"][:, k, :], lambda k: B["oL"][:, k, :])
            E.arrive()
            products("ba", 1, h_hi, h_lo)
            emptied(E, TILE["ba"])
            for t in range(TB):
                mm = turn(ps[5][:, t * P:(t + 1) * P], tmp[:, 0, t * P:(t + 1) * P])
            mm.then_inc(sems("ba_turned"), 1)
            products("gdn_qkv", 8, h_hi, h_lo)
            E.wait("g_ready")
            pe.matmul(ps[6][:, 0:32], C("upi"), B["ga"][:, 1], start=True, stop=True)
            pe.matmul(ps[6][:, 32:64], ones, B["ga"][:, 1], start=True, stop=True).then_inc(sems("g_sums"), 1)
            tiles_beside_norm("gdn_qkv", 8)
            tiles_beside_norm("gdn_qkv", 16)
            E.meet()
            for tb in range(TB):
                ts = slice(tb * P, (tb + 1) * P)
                E.at("gd_end", 2 * tb)
                for c in range(2):
                    g = G[c]
                    E.at("gd_setup", 2 * tb + c)
                    for x in range(4):
                        turn(ps[0][:, col(x)], B["gk"][:, 4 * c + x, ts])
                    for x in range(4):
                        mm = turn(ps[1][:, col(x)], B["gv"][:, 4 * c + x, ts])
                    mm.then_inc(sems("gd_turned"), 1)
                    for y in range(2):
                        E.wait("gd_diag")
                        pe.matmul(ps[4 + y][:, :], ones, dg[:, y, :], start=True, stop=True).then_inc(sems("gd_rows"), 1)
                    for x in range(4):
                        pe.matmul(ps[2][:, col(x)], B["gk"][:, 4 * c + x, ts], B["gk"][:, 4 * c + x, ts], start=True, stop=True)
                    for x in range(4):
                        mm = pe.matmul(ps[3][:, col(x)], B["gk"][:, 4 * c + x, ts], B["gq"][:, 4 * c + x, ts], start=True, stop=True)
                    mm.then_inc(sems("gd_kk"), 1)
                for lv in range(LEVELS):
                    for c in range(2):
                        g = G[c]
                        E.wait("gd_N")
                        if lv == 0 and c == 1:
                            E.at("gd_setup", 2 * tb + 2)
                        if lv:
                            E.wait("gd_T")
                            E.at("gd_R", 14 * tb + 2 * (lv - 1) + c + 1)
                        for x in range(4):
                            mm = pe.matmul(ps[X_BANK[c]][:, col(x)], g["N"][:, x], g["T"][:, x] if lv else ident,
                                           start=True, stop=True)
                        mm.then_inc(sems("gd_X"), 1)
                    for c in range(2 if lv else 0):
                        g = G[c]
                        E.wait("gd_Xc")
                        if lv < LEVELS - 1:
                            for x in range(4):
                                mm = pe.matmul(ps[Y_BANK[c]][:, col(x)], g["R"][:, x], g["X"][:, x], start=True, stop=True)
                            mm.then_inc(sems("gd_Y"), 1)
                        for x in range(4):
                            mm = pe.matmul(ps[X_BANK[c]][:, col(x)], g["X"][:, x], g["R"][:, x], start=True, stop=True)
                        mm.then_inc(sems("gd_YT"), 1)
                for c in range(2):
                    for x in range(4):
                        mm = pe.matmul(ps[c][:, col(x)], B["gk"][:, 4 * c + x, ts], B["state"][:, 4 * c + x], start=True, stop=True)
                    mm.then_inc(sems("gd_kS"), 1)
                for c in range(2):
                    g = G[c]
                    E.wait("gd_rhs")
                    for x in range(4):
                        mm = pe.matmul(ps[2 + c][:, col(x)], g["R"][:, x], g["N"][:, x], start=True, stop=True)
                    mm.then_inc(sems("gd_v"), 1)
                for c in range(2):
                    g = G[c]
                    E.wait("gd_vc")
                    for x in range(4):
                        pe.matmul(ps[4 + c][:, col(x)], B["state"][:, 4 * c + x], g["er"][:, x], start=True, stop=False)
                        mm = pe.matmul(ps[4 + c][:, col(x)], g["X"][:, x], g["aT"][:, x], start=False, stop=True)
                    mm.then_inc(sems("gd_o"), 1)
                    for x in range(4):
                        mm = pe.matmul(ps[6 + c][:, col(x)], g["kw"][:, x], g["X"][:, x], start=True, stop=True)
                    mm.then_inc(sems("gd_S"), 1)
            E.arrive()
            tiles_beside_norm("z")
            products("gate_gdn", 8, h_hi, h_lo)
            E.at("gz_done", 8)
            products("branch_gdn", 8, lambda k: B["goH"][:, k, :], lambda k: B["goL"][:, k, :])
            E.arrive()
            products_and_sums("out2", ready=lambda k: E.wait("merged_parts"))
            norm_pe(E, summed=True, **NORMS["ffn2"])
            E.arrive()
            products("wq", 16, h_hi, h_lo, ready=parts_ready)
            E.meet()
            t0 = TILE["peer"]
            pe.wait_ge(sems("keys_in"), 16)

            def key_scores(u):
                tb, h = u // 8, u % 8
                E.at("tk_read", 2 * (u - 1))
                for c in range(2):
                    mm = pe.matmul(ps[2 + u % 2][:, c * P:(c + 1) * P], B["qp"][:, 2 * h + c, tb * P:(tb + 1) * P],
                                   B["keys"][:, 2 * h + c, :], start=True, stop=True)
                mm.then_inc(sems("tk_scores"), 1)

            n = 0
            key_scores(0)
            for u in range(32):
                if u + 1 < 32:
                    key_scores(u + 1)
                for _ in range(5 if u % 8 == 7 else 1):
                    one_tile(t0 + n, h_hi, h_lo)
                    n += 1
                if u % 8 == 7:
                    for c in range(3):
                        E.wait("tk_expert")
                        E.at("slots_copied", 3 * (u // 8) + c)
                        turn(ps[4][:, 0:P], B["eg"][:, c]).then_inc(sems("slots_turned"), 1)
            E.meet()
            E.prime("gb_product")
            with pe.Fori(0, TG) as j:
                for r in range(8):
                    pe.wait_ge(sems("gb_rows"), 8 * j + (r + 1))
                    pe.wait_ge(sems("gb_copied"), 8 * j + max(r - 2, 1))
                    for x in range(4):
                        mm = pe.matmul(ps[2 + r % 4][:, x * P:(x + 1) * P], B["gated"][:, r % 4, x], B["onehot"][:, r % 4, x],
                                       start=True, stop=True)
                    mm.then_inc(sems("gb_product"), 1)
                    if r % 4 == 3:
                        one_tile(t0 + n + r // 4, h_hi, h_lo, S, j, 2)
            E.arrive()

            def v_tile(t, z, before, j, step, per_turn):
                def weighed(k):
                    if before is not None:
                        m = before + k + 2
                        pe.wait_ge(sems("pz_ready"), m + per_turn * j)
                one_tile(t, lambda k: B["pzH"][:, z, k, :], lambda k: B["pzL"][:, z, k, :], S, j, step, ready=weighed)

            t0 += 8 * EARLY
            with pe.Fori(0, LATE) as j:
                for e in range(8):
                    one_tile(t0 + e, h_hi, h_lo, S, j, 16)
                for d in range(8):
                    v_tile(t0 + 8 + d, 0, 0 if d == 0 else None, j, 16, 8)
            t0 += 16 * LATE
            with pe.Fori(0, EARLY // 2) as j:
                for i in range(2):
                    for d in range(8):
                        v_tile(t0 + 8 * i + d, 1 - i, 8 * (LATE + i) if d == 0 else None, j, 16, 16)
            E.meet()

        def second_act(E, eng, copy_tiles, squares_behind):
            if not first:
                eng.wait_ge(sems("x_in"), 16)

            def normed(k):
                if first and k < KB - 1:
                    E.wait("x_normed")
                elif first:
                    E.at("rb_used", 1 + 1 + 4 + 1 + 1 + 1 + 1)

            norm_act(E, when=normed, **NORMS["mix2"])
            E.meet()
            copy_tiles("sb_qkv", 8, lambda b: B["sbq"][:, b, :])
            for at, name, norm in ((8, "sbk", "sb_q"), (16, "sbv", "sb_k")):
                emptied(E, TILE["sb_qkv"] + at - 2)
                emptied(E, TILE["sb_qkv"] + at - 1)
                for b in range(8):
                    norm_beside_act(E, b, NORMS[norm]["src"])
                    copy_tiles("sb_qkv", 1, lambda _: B[name][:, b, :], at=at + b)
                    if b == 3:
                        root_act(E, 8 * TB)
            E.meet()
            for h in range(NH2 + 2):
                if h < NH2:
                    t_all = sb_t[h % 2]
                    E.at("sb_a", TB * (h - 1))
                    for kb in reversed(range(TB)):
                        E.wait("sb_z")
                        act.activation(t_all[:, offs[kb]:offs[kb] + qw[kb]], ps[4 + kb][:, 0:qw[kb]], ACT.Abs).then_inc(sems("sb_step"), 1)
                    E.wait("sb_step", 4)
                    act.activation(t_all, t_all, ACT.Exp, scale=-1.0).then_inc(sems("sb_step"), 1)
                    E.wait("sb_step")
                    act.activation(t_all, t_all, ACT.Ln, bias=1.0).then_inc(sems("sb_t"), 1)
                if h >= 2:
                    E.wait("sb_o")
                    act.activation(B["sbq"][:, h - 2, :], ps[3][:, :], ACT.Copy).then_inc(sems("sb_o_copied"), 1)
                if 1 <= h <= NH2:
                    for kb in reversed(range(TB)):
                        E.wait("sb_la")
                        E.at("sb_o", h - 2)
                        o = slice(offs[kb], offs[kb] + qw[kb])
                        act.activation(sb_a[(h - 1) % 2][:, o], sb_t[(h - 1) % 2][:, o], ACT.Exp).then_inc(sems("sb_a"), 1)
            E.meet()
            for h in range(NH2):
                act.activation(B["oH"][:, h, :], B["sbq"][:, h, :], ACT.Copy).then_inc(sems("hi_ready"), 1)
            E.meet()
            copy_tiles("gate_sb", 8, lambda b: B["merged"][:, b, :], func=ACT.Sigmoid)
            E.meet()
            copy_tiles("ba", 1, lambda b: tmp[:, 0, :])
            ga = lambda n: B["ga"][:, n]
            E.wait("ba_raw")
            act.activation(ga(0), ga(8), ACT.Sigmoid).then_inc(sems("ga_act"), 1)
            act.activation(ga(2), ga(9), ACT.Abs).then_inc(sems("ga_step"), 1)
            E.wait("ga_step")
            act.activation(ga(2), ga(2), ACT.Exp, scale=-1.0).then_inc(sems("ga_step"), 1)
            E.wait("ga_step")
            act.activation(ga(2), ga(2), ACT.Ln, bias=1.0)
            act.activation(sc[:, 8:16], PM("a_log", 0, 8), ACT.Exp).then_inc(sems("ga_act"), 1)
            for i in range(25):
                if i == 9:
                    E.wait("gc_ready")
                    act.activation(ga(3), ga(2), ACT.Exp)
                    act.activation(ga(6), ga(5), ACT.Exp)
                    act.activation(ga(7), ga(4), ACT.Exp).then_inc(sems("ga_act"), 1)
                if 8 <= i < 24:
                    if i % 8 < 4:
                        E.at("g_silu", i // 8 * 8 - 8 + 2 * (i % 8) + 2)
                    norm_beside_act(E, i % 8, NORMS["l2_q" if i < 16 else "l2_k"]["src"])
                if i < 24:
                    t = TILE["gdn_qkv"] + i
                    tile_ready(E, t)
                    E.at("gconv", i - 3)
                    empties(act.activation(B["gpad"][:, i % 4, 3:S + 3], bank(t), ACT.Copy), t)
                if 8 <= i < 24 and i % 8 == 3:
                    root_act(E, 8 * TB)
                if 1 <= i <= 24:
                    E.at("gconv", i)
                    to = B[("gq", "gk", "gv")[(i - 1) // 8]][:, (i - 1) % 8, :]
                    act.activation(to, to, ACT.Silu).then_inc(sems("g_silu"), 1)
            E.meet()
            bank4 = lambda m: ps[m][:, :].rearrange("p (x t) -> p x t", x=4)
            for tb in range(TB):
                for c in range(2):
                    g = G[c]
                    E.at("gd_rows", 2 * (2 * tb + c) + 1)
                    E.at("gd_end", 2 * tb)
                    act.activation(g["er"], bank4(4), ACT.Exp).then_inc(sems("gd_er"), 1)
                    E.wait("gd_dT")
                    act.activation(g["X"], g["X"], ACT.Exp).then_inc(sems("gd_dTe"), 1)
                for lv in range(1, LEVELS):
                    for c in range(2):
                        E.at("gd_X", 14 * tb + 2 * lv + c + 1)
                        act.activation(G[c]["X"], bank4(X_BANK[c]), ACT.Copy).then_inc(sems("gd_Xc"), 1)
                for c in range(2):
                    E.wait("gd_v")
                    act.activation(G[c]["X"], bank4(2 + c), ACT.Copy).then_inc(sems("gd_vc"), 1)
            E.meet()
            for b in range(9):
                if b < 8:
                    norm_beside_act(E, b, NORMS["gdn"]["src"])
                    copy_tiles("z", 1, lambda _: B["gg"][:, b, :], at=b, func=ACT.Silu)
                if b == 3:
                    root_act(E, 8 * TB)
                for g in (2 * b - 10, 2 * b - 9) if b >= 5 else ():
                    E.at("gz", g + 1)
                    act.activation(B["goH"][:, g, :], B["gq"][:, g, :], ACT.Copy).then_inc(sems("hi_ready"), 1)
            copy_tiles("gate_gdn", 8, lambda b: B["gg"][:, b, :], func=ACT.Sigmoid)
            for b in range(8):
                E.wait("merged")
                act.activation(hH[:, b, :], B["merged"][:, b, :], ACT.Copy).then_inc(sems("hi_ready"), 1)
            E.meet()
            squares_behind("out2")
            norm_act(E, squared=True, **NORMS["ffn2"])
            eng.dma_start(B["keys"][:], a["keys"].rearrange("n d k -> d n k")).then_inc(sems("keys_in"), 16)
            E.meet()
            copy_tiles("wq", 16, lambda b: B["qp"][:, b, :])
            E.meet()
            t0 = TILE["peer"]

            def early_gelu(n, slot, used, at, j=None, per=0):
                t = t0 + n
                tile_ready(E, t, j, per)
                if j is not None or used:
                    eng.wait_ge(sems(f"spilled{slot}"), 16 * used if j is None else 16 * used + 16 * j)
                act.activation(sq[:, slot, :], bank(t), ACT.Gelu).then_inc(sems(f"bank_free{t % 2}"), 1)
                emptied(E, t, j, per)
                eng.dma_start(at, sq[:, slot, :]).then_inc(sems(f"spilled{slot}"), 16)

            n = 0
            for u in range(32):
                for _ in range(5 if u % 8 == 7 else 1):
                    early_gelu(n, n % 4, n // 4, acts[n])
                    n += 1
                if u % 8 == 7:
                    tb = u // 8
                    E.wait("tk_centred")
                    act.activation(B["cv"][:], B["cv"][:], ACT.Exp).then_inc(sems("tk_exp"), 1)
                    for c in range(3):
                        E.wait("slots_turned")
                        act.activation(B["slots"][:, c, tb * P:(tb + 1) * P], ps[4][:, 0:P], ACT.Copy).then_inc(sems("slots_copied"), 1)
            E.meet()
            E.prime("gb_copied")
            for jj in range(2):
                E.prime(f"stage_out{jj}", 16)
            acts4 = acts.rearrange("(a b) p t -> a b p t", b=4)
            with eng.Fori(0, TG // 2) as j:
                for jj in range(2):
                    for r in range(8):
                        eng.wait_ge(sems("gb_product"), 16 * j + (8 * jj + r + 2))
                        if r == 0:
                            eng.wait_ge(sems(f"stage_out{jj}"), 16 * j + 16)
                        ins = act.activation(B["stage"][:, jj, :, 4 * r:4 * r + 4].rearrange("p e t -> p t e"),
                                             ps[2 + r % 4][:, :].rearrange("p (t e) -> p t e", t=4), ACT.Copy)
                        ins.then_inc(sems("gb_copied"), 1)
                        if r % 4 == 3:
                            b = 2 * jj + r // 4
                            early_gelu(n + b, b, n // 4, acts4[bass.ds(j + n // 4, 1), b].rearrange("o p t -> p (o t)"), j, 2)
                    eng.wait_ge(sems("gb_copied"), 16 * j + (8 * jj + 9))
                    eng.dma_start(gates.rearrange("(j s) p e t -> j s p (e t)", s=2)[bass.ds(j, 1), jj].rearrange("o p f -> p (o f)"),
                                  B["stage"][:, jj].rearrange("p e t -> p (e t)")).then_inc(sems(f"stage_out{jj}"), 16)
            for jj in range(2):
                eng.wait_ge(sems(f"stage_out{jj}"), 16 * (TG // 2) + 16)
            for b in range(4):
                eng.wait_ge(sems(f"spilled{b}"), 16 * 2 * EARLY)
            E.meet()
            t0 += 8 * EARLY
            by_group = gates.rearrange("g p (n e) t -> n p g (e t)", e=8)
            with eng.Fori(0, LATE) as j:
                eng.wait_ge(sems("pz_v"), 8 * j + 1)
                eng.dma_start(B["Gt"][:], by_group[bass.ds(j + EARLY, 1)].rearrange("o p g f -> p (o g) f")).then_inc(
                    sems("gates_in"), 16)
                for e in range(8):
                    t = t0 + e
                    tile_ready(E, t, j, 8)
                    n = 8 * j + e
                    if e >= 2:
                        eng.wait_ge(sems("pz_v"), n)
                    act.activation(sq[:, e % 2, :], bank(t), ACT.Gelu).then_inc(sems(f"bank_free{t % 2}"), 1)
                    if e >= 1:
                        eng.wait_ge(sems("pz_v"), n + 1)
                        act.activation(B["pzH"][:, 0, e - 1, :], tmp[:, (e - 1) % 4, :], ACT.Copy).then_inc(sems("pz_hi"), 1)
                eng.wait_ge(sems("pz_v"), 8 * j + 9)
                act.activation(B["pzH"][:, 0, 7, :], tmp[:, 3, :], ACT.Copy).then_inc(sems("pz_hi"), 1)

            gh = gates.rearrange("g p (n f e) t -> n f p g (e t)", f=2, e=4)
            ah = acts.rearrange("(n f e) p t -> n f p e t", f=2, e=4)

            def load_half(i, f, j=None):
                m = 8 * (LATE + i - 1) + 4 * f + 4 + 1
                eng.wait_ge(sems("pz_v"), m if j is None else m + 16 * j)
                gsrc = gh[i, f] if j is None else gh[bass.ds(2 * j + i, 1), f].rearrange("o p g x -> p (o g) x")
                asrc = ah[i, f] if j is None else ah[bass.ds(2 * j + i, 1), f].rearrange("o p e t -> p (o e) t")
                eng.dma_start(B["Gt"][:, :, 4 * f:4 * f + 4, :].rearrange("p g e t -> p g (e t)"), gsrc).then_inc(sems(f"half_in{f}"), 16)
                eng.dma_start(B["Ga"][:, 4 * f:4 * f + 4, :], asrc).then_inc(sems(f"half_in{f}"), 16)

            def early_hi(i, j=None, load=None):
                for e in range(8):
                    m = 8 * (LATE + i) + e + 2
                    eng.wait_ge(sems("pz_v"), m if j is None else m + 16 * j)
                    act.activation(B["pzH"][:, (i + 1) % 2, e, :], tmp[:, e % 4, :], ACT.Copy).then_inc(sems("pz_hi"), 1)
                    if load is not None and e % 4 == 3:
                        load_half(load, e // 4, j)

            load_half(0, 0)
            load_half(0, 1)
            early_hi(0, None, 1)
            with eng.Fori(0, EARLY // 2 - 1) as j:
                early_hi(1, j, 2)
                early_hi(2, j, 3)
            early_hi(EARLY - 1)
            E.meet()

        def second_dve(E, eng, chain, add_tiles):
            chain(v.tensor_scalar(sc[:, 5:6], PM("sbq"), P ** -0.5, None, ALU.mult))
            if not first:
                eng.wait_ge(sems("x_in"), 16)
            norm_dve(E, chain, **NORMS["mix2"])
            E.meet()
            for b in range(8):
                norm_beside_dve(E, chain, b, **NORMS["sb_q"])
            for b in range(9):
                if b < 8:
                    norm_beside_dve(E, chain, b, **NORMS["sb_k"])
                if b:
                    E.wait("sbv_turn")
                    v.tensor_copy(B["sbvt"][:, :, (b - 1) * P:b * P],
                                  ps[5 + (b - 1) % 2][:, :].rearrange("p (t d) -> p t d", t=TB)).then_inc(sems("sbv_turned"), 1)
            E.meet()
            for h in range(NH2 + 1):
                if h < NH2:
                    E.wait("sb_t")
                    for kb in reversed(range(TB)):
                        o = slice(offs[kb], offs[kb] + qw[kb])
                        d = slice(offs[kb], offs[kb] + P)
                        z, t_z = ps[4 + kb][:, 0:qw[kb]], sb_t[h % 2][:, o]
                        E.at("sb_S", TB * h)
                        chain(v.scalar_tensor_tensor(out=B["Lp"][:, o], in0=z, scalar=0.0, in1=t_z, op0=ALU.max, op1=ALU.add))
                        v.scalar_tensor_tensor(out=t_z, in0=z, scalar=0.0, in1=t_z, op0=ALU.min, op1=ALU.subtract).then_inc(sems("sb_ls"), 1)
                        v.tensor_tensor(B["Lp"][:, d], B["Lp"][:, d], C("ups"), ALU.mult).then_inc(sems("sb_L"), 1)
                if h >= 1:
                    for kb in reversed(range(TB)):
                        d = slice(offs[kb], offs[kb] + P)
                        E.wait("sb_a")
                        w_d = sb_a[(h - 1) % 2][:, d]
                        v.tensor_tensor(w_d, w_d, C("ups"), ALU.mult).then_inc(sems("sb_am"), 1)
                if h < NH2:
                    for kb in reversed(range(TB)):
                        l_a = sb_t[h % 2][:, offs[kb]:offs[kb] + qw[kb]]
                        E.at("sb_ls", TB * h + TB - kb)
                        E.wait("sb_S")
                        v.tensor_tensor(l_a, l_a, ps[kb][:, 0:qw[kb]], ALU.subtract).then_inc(sems("sb_la"), 1)
            E.meet()
            for h in range(NH2):
                E.wait("hi_ready")
                v.tensor_tensor(B["oL"][:, h, :], B["sbq"][:, h, :], B["oH"][:, h, :].bitcast(F32), ALU.subtract).then_inc(sems("sb_o_parts"), 1)
            E.meet()
            for b in range(8):
                t = TILE["branch_sb"] + b
                tile_ready(E, t)
                emptied(E, TILE["gate_sb"] + b)
                empties(v.tensor_tensor(B["merged"][:, b, :], B["merged"][:, b, :], bank(t), ALU.mult), t)
            E.meet()
            chain(v.memset(B["gpad"][:, :, 0:3], 0.0))
            ga = lambda n: B["ga"][:, n]
            E.wait("ba_turned")
            bt = ps[5][:, :].rearrange("p (t c) -> p t c", t=TB)
            chain(v.tensor_copy(ga(8), bt[:, :, 0:8]))
            v.tensor_tensor(ga(9), bt[:, :, 8:16], PM("dt", 0, 8).unsqueeze(1).to_broadcast([P, TB, 8]), ALU.add).then_inc(sems("ba_raw"), 1)
            E.wait("ga_act", 2)
            E.at("ba_raw", 1)
            chain(v.scalar_tensor_tensor(out=ga(9), in0=ga(9), scalar=0.0, in1=ga(2), op0=ALU.max, op1=ALU.add))
            v.scalar_tensor_tensor(out=ga(1), in0=ga(9), scalar=-1.0, in1=sc[:, 8:16].unsqueeze(1).to_broadcast([P, TB, 8]),
                                   op0=ALU.mult, op1=ALU.mult).then_inc(sems("g_ready"), 1)
            for i in range(24):
                if i == 8:
                    E.wait("g_sums")
                    sums = lambda n: ps[6][:, 32 * n:32 * n + 32].rearrange("p (t h) -> p t h", t=TB)
                    chain(v.tensor_copy(ga(2), sums(0)))
                    chain(v.tensor_copy(ga(4), sums(1)))
                    v.tensor_tensor(ga(5), ga(4), ga(2), ALU.subtract).then_inc(sems("gc_ready"), 1)
                if i >= 8:
                    norm_beside_dve(E, chain, i % 8, **NORMS["l2_q" if i < 16 else "l2_k"])
                emptied(E, TILE["gdn_qkv"] + i)
                u = B["gpad"][:, i % 4, :]
                to = B[("gq", "gk", "gv")[i // 8]][:, i % 8, :]
                w = lambda k: PM("gdn_w", 4 * i + k)
                chain(v.tensor_scalar(to, u[:, 0:S], w(0), None, ALU.mult))
                for k in range(1, 4):
                    ins = v.scalar_tensor_tensor(out=to, in0=u[:, k:S + k], scalar=w(k), in1=to, op0=ALU.mult, op1=ALU.add)
                    if k < 3:
                        chain(ins)
                ins.then_inc(sems("gconv"), 1)
            E.wait("ga_act")
            chain(v.scalar_tensor_tensor(out=ga(8), in0=ga(3), scalar=-1.0, in1=ga(0), op0=ALU.mult, op1=ALU.mult))
            chain(v.memset(B["state"][:], 0.0))
            E.meet()
            bc = [P, 4, P]
            bank4 = lambda m: ps[m][:, :].rearrange("p (x t) -> p x t", x=4)
            d4 = lambda m: dg[:, m, :].rearrange("p (x t) -> p x t", x=4)
            wide = lambda ap: ap.unsqueeze(1).to_broadcast(bc)
            for tb in range(TB):
                ts = slice(tb * P, (tb + 1) * P)
                gs = lambda m, c: B["ga"][:, m, tb, 4 * c:4 * c + 4].unsqueeze(2).to_broadcast(bc)

                def next_level(c, lv):
                    g = G[c]
                    v.tensor_tensor(g["N"], g["LT"], wide(C("levels", lv * P, P)), ALU.mult).then_inc(sems("gd_N"), 1)

                for c in range(2):
                    g = G[c]
                    h = slice(4 * c, 4 * c + 4)
                    E.at("gd_rows", 2 * (2 * tb + c))
                    v.tensor_tensor(d4(0), wide(C("upi")), gs(1, c), ALU.mult).then_inc(sems("gd_diag"), 1)
                    v.tensor_tensor(d4(1), wide(ident), gs(0, c), ALU.mult).then_inc(sems("gd_diag"), 1)
                    E.wait("gd_er")
                    chain(v.tensor_tensor(g["X"], bank4(4), gs(2, c), ALU.subtract))
                    v.tensor_scalar(g["X"], g["X"], 0.0, None, ALU.min).then_inc(sems("gd_dT"), 1)
                    E.wait("gd_turned")
                    chain(v.tensor_tensor(g["kw"], bank4(0), gs(6, c), ALU.mult))
                    chain(v.tensor_tensor(g["vb"], bank4(1), gs(0, c), ALU.mult))
                    chain(v.tensor_tensor(g["er"], g["er"], B["gq"][:, h, ts], ALU.mult))
                    E.wait("gd_kk")
                    E.wait("gd_dTe")
                    chain(v.tensor_tensor(g["LT"], bank4(2), g["X"], ALU.mult))
                    chain(v.tensor_tensor(g["aT"], bank4(3), g["X"], ALU.mult))
                    chain(v.tensor_tensor(g["LT"], g["LT"], wide(C("ups")), ALU.mult))
                    chain(v.tensor_tensor(g["aT"], g["aT"], wide(C("upi")), ALU.mult))
                    E.at("gd_rows", 2 * (2 * tb + c) + 2)
                    v.tensor_tensor(g["LT"], g["LT"], bank4(5), ALU.mult).then_inc(sems("gd_setup"), 1)
                    E.wait("gd_setup")
                    next_level(c, 0)
                for lv in range(LEVELS):
                    for c in range(2):
                        g = G[c]
                        E.at("gd_X", 14 * tb + 2 * lv + c + 1)
                        if lv == 0:
                            v.tensor_tensor(g["T"], wide(ident), bank4(X_BANK[c]), ALU.subtract).then_inc(sems("gd_T"), 1)
                            v.tensor_tensor(g["R"], wide(ident), g["N"], ALU.subtract).then_inc(sems("gd_R"), 1)
                            E.at("gd_R", 14 * tb + c + 1)
                        if lv < LEVELS - 1:
                            next_level(c, lv + 1)
                    for c in range(2 if lv else 0):
                        g = G[c]
                        if lv < LEVELS - 1:
                            E.wait("gd_Y")
                            v.tensor_tensor(g["T"], g["T"], bank4(Y_BANK[c]), ALU.subtract).then_inc(sems("gd_T"), 1)
                        E.wait("gd_YT")
                        v.tensor_tensor(g["R"], g["R"], bank4(X_BANK[c]), ALU.subtract).then_inc(sems("gd_R"), 1)
                for c in range(2):
                    g = G[c]
                    E.wait("gd_kS")
                    chain(v.tensor_tensor(g["N"], bank4(c), gs(8, c), ALU.mult))
                    v.tensor_tensor(g["N"], g["N"], g["vb"], ALU.add).then_inc(sems("gd_rhs"), 1)
                for c in range(2):
                    h = slice(4 * c, 4 * c + 4)
                    E.wait("gd_o")
                    chain(v.tensor_copy(B["gq"][:, h, ts], bank4(4 + c)))
                    E.wait("gd_S")
                    st8 = B["state"][:, h]
                    chain(v.tensor_tensor(st8, st8, gs(7, c), ALU.mult))
                    v.tensor_tensor(st8, st8, bank4(6 + c), ALU.add).then_inc(sems("gd_end"), 1)
            E.meet()
            def gated_lo(g):
                E.wait("hi_ready")
                v.tensor_tensor(B["goL"][:, g, :], B["gq"][:, g, :], B["goH"][:, g, :].bitcast(F32), ALU.subtract).then_inc(sems("gz_done"), 1)

            for b in range(8):
                norm_beside_dve(E, chain, b, **NORMS["gdn"])
                for g in (2 * b - 8, 2 * b - 7) if b >= 4 else ():
                    if g >= 2:
                        gated_lo(g - 2)
                    if g % 2 == 0:
                        E.at("rb_used", E.n["made rbr"])
                    emptied(E, TILE["z"] + g)
                    v.tensor_tensor(B["gq"][:, g, :], B["gq"][:, g, :], B["gg"][:, g, :], ALU.mult).then_inc(sems("gz"), 1)
            gated_lo(6)
            gated_lo(7)
            def merged_lo(b):
                E.wait("hi_ready")
                v.tensor_tensor(hL[:, b, :], B["merged"][:, b, :], hH[:, b, :].bitcast(F32), ALU.subtract).then_inc(sems("merged_parts"), 1)

            for b in range(8):
                t = TILE["branch_gdn"] + b
                tile_ready(E, t)
                emptied(E, TILE["gate_gdn"] + b)
                empties(v.tensor_tensor(tmp[:, b % 4, :], bank(t), B["gg"][:, b, :], ALU.mult), t)
                emptied(E, t)
                v.tensor_tensor(B["merged"][:, b, :], B["merged"][:, b, :], tmp[:, b % 4, :], ALU.add).then_inc(sems("merged"), 1)
                if b:
                    merged_lo(b - 1)
            merged_lo(7)
            E.meet()
            add_tiles("out2")
            norm_dve(E, chain, **NORMS["ffn2"])
            E.meet()
            E.meet()
            u8 = lambda o: slice(8 * o, 8 * o + 8)
            for u in range(32):
                tb, h = u // 8, u % 8
                E.wait("tk_scores")
                for c in range(2):
                    s = ps[2 + u % 2][:, c * P:(c + 1) * P]
                    vals, idx = B["v12"][:, c], B["i12"][:, h, c]
                    wk = B["work"][:, c * P:(c + 1) * P]
                    chain(v.max(vals[:, u8(0)], s))
                    chain(v.max_index(idx[:, u8(0)], vals[:, u8(0)], s))
                    v.match_replace(wk, vals[:, u8(0)], s, NEG * 1e8).then_inc(sems("tk_read"), 1)
                    E.at("tk_read", 2 * u + c + 1)
                    chain(v.max(vals[:, u8(1)], wk))
                    chain(v.max_index(idx[:, u8(1)], vals[:, u8(1)], wk))
                cand = B["cand"][:].rearrange("p (i j) -> p i j", i=16)
                chain(v.tensor_tensor(cand, B["v12"][:, 0].unsqueeze(2).to_broadcast([P, 16, 16]),
                                      B["v12"][:, 1].unsqueeze(1).to_broadcast([P, 16, 16]), ALU.add))
                cv, ci = B["cv"][:, h], B["ci"][:, h]
                if h == 0 and tb:
                    E.at("slots_turned", 3 * tb)
                chain(v.max(cv[:, u8(0)], B["cand"][:]))
                chain(v.max_index(ci[:, u8(0)], cv[:, u8(0)], B["cand"][:]))
                chain(v.match_replace(B["work"][:], cv[:, u8(0)], B["cand"][:], NEG * 1e8))
                chain(v.max(cv[:, u8(1)], B["work"][:]))
                chain(v.max_index(ci[:, u8(1)], cv[:, u8(1)], B["work"][:]))
                if h < 7:
                    continue
                chain(v.tensor_single_scalar(B["cc"][:, 0], B["ci"][:], 4, ALU.logical_shift_right))
                chain(v.tensor_single_scalar(B["cc"][:, 1], B["ci"][:], 15, ALU.bitwise_and))
                chain(v.tensor_copy(B["cf"][:], B["cc"][:]))
                chain(v.tensor_copy(B["if12"][:], B["i12"][:]))
                eq = B["eq"][:].rearrange("p (n i) -> p n i", i=16)
                for c in range(2):
                    E.at("tk_expert", 3 * tb + c)
                    chain(v.tensor_tensor(eq, B["cf"][:, c].rearrange("p h s -> p (h s)").unsqueeze(2).to_broadcast([P, P, 16]),
                                          C("iota", 0, 16).unsqueeze(1).to_broadcast([P, P, 16]), ALU.is_equal))
                    e4 = B["eq"][:].rearrange("p (h s i) -> p h s i", h=8, i=16)
                    chain(v.tensor_tensor(e4, e4, B["if12"][:, :, c].unsqueeze(2).to_broadcast([P, 8, 16, 16]), ALU.mult))
                    v.tensor_reduce(B["eg"][:, c], eq, AX, ALU.add).then_inc(sems("tk_expert"), 1)
                cvs = B["cv"][:]
                chain(v.tensor_copy(B["eg"][:, 3, 0:8], B["cv"][:, :, 0]))
                v.tensor_tensor(cvs, cvs, B["eg"][:, 3, 0:8].unsqueeze(2).to_broadcast([P, 8, 16]), ALU.subtract).then_inc(sems("tk_centred"), 1)
                E.wait("tk_exp")
                chain(v.tensor_reduce(B["eg"][:, 3, 8:16], cvs, AX, ALU.add))
                chain(v.reciprocal(B["eg"][:, 3, 16:24], B["eg"][:, 3, 8:16]))
                v.tensor_tensor(B["eg"][:, 2].rearrange("p (h s) -> p h s", h=8), cvs,
                                         B["eg"][:, 3, 16:24].unsqueeze(2).to_broadcast([P, 8, 16]), ALU.mult).then_inc(sems("tk_expert"), 1)
            E.meet()
            with eng.Fori(0, TG) as j:
                e1 = B["slots"][:, 0].rearrange("p (j r x) -> p j r x", j=TG, x=4)
                for r in range(8):
                    eng.wait_ge(sems("gb_product"), 8 * j + max(r - 2, 1))
                    v.tensor_tensor(B["onehot"][:, r % 4], C("iota").unsqueeze(1).to_broadcast(bc),
                                    e1[:, bass.ds(j, 1), r].rearrange("p o x -> p (o x)").unsqueeze(2).to_broadcast(bc), ALU.is_equal)
                    for x in range(4):
                        at = lambda c: B["slots"][:, c].rearrange("p (j n) -> p j n", j=TG)[:, bass.ds(j, 1), 4 * r + x]
                        ins = v.tensor_scalar(B["gated"][:, r % 4, x], C("iota"), at(1), at(2), ALU.is_equal, ALU.mult)
                    ins.then_inc(sems("gb_rows"), 1)
            E.meet()
            t0 = TILE["peer"] + 8 * EARLY
            E.prime("pz_v")
            E.prime("pz_ready")
            by_tg = lambda ap: ap.rearrange("p (g t) -> p g t", g=TG)
            with eng.Fori(0, LATE) as j:
                eng.wait_ge(sems("gates_in"), 16 * j + 16)
                eng.wait_ge(sems("pz_ready"), 8 * j + 1)
                for e in range(9):
                    n = 8 * j + e
                    if e < 8:
                        emptied(E, t0 + e, j, 8)
                        if e >= 4:
                            eng.wait_ge(sems("pz_ready"), n - 2)
                        v.tensor_tensor(by_tg(tmp[:, e % 4, :]), by_tg(sq[:, e % 2, :]), B["Gt"][:, :, e, :],
                                        ALU.mult).then_inc(sems("pz_v"), 1)
                    if e >= 1:
                        eng.wait_ge(sems("pz_hi"), n)
                        v.tensor_tensor(B["pzL"][:, 0, e - 1, :], tmp[:, (e - 1) % 4, :], B["pzH"][:, 0, e - 1, :].bitcast(F32),
                                        ALU.subtract).then_inc(sems("pz_ready"), 1)
                for d in range(8):
                    t = t0 + 8 + d
                    tile_ready(E, t, j, 8)
                    v.tensor_tensor(xT[:, d, :], xT[:, d, :], bank(t), ALU.add).then_inc(sems(f"bank_free{t % 2}"), 1)

            t0 += 16 * LATE

            def early_group(i, z, j=None):
                plus = lambda m, per: m if j is None else m + per * j
                for e in range(9):
                    if i is not None and e < 8:
                        t = t0 + 8 * i + e
                        tile_ready(E, t, j, 8)
                        v.tensor_tensor(xT[:, e, :], xT[:, e, :], bank(t), ALU.add).then_inc(sems(f"bank_free{t % 2}"), 1)
                    if z is None:
                        continue
                    m = 8 * (LATE + z) + e
                    if e < 8:
                        eng.wait_ge(sems(f"half_in{e // 4}"), plus(32 * (z + 1), 64))
                        eng.wait_ge(sems("pz_ready"), plus(m - 2, 16))
                        if e == 0:
                            tile_ready(E, t0 + 8 * (z - 2) + 7, j, 8)
                        v.tensor_tensor(by_tg(tmp[:, e % 4, :]), by_tg(B["Ga"][:, e, :]), B["Gt"][:, :, e, :],
                                        ALU.mult).then_inc(sems("pz_v"), 1)
                    if e >= 1:
                        eng.wait_ge(sems("pz_hi"), plus(m, 16))
                        v.tensor_tensor(B["pzL"][:, (z + 1) % 2, e - 1, :], tmp[:, (e - 1) % 4, :],
                                        B["pzH"][:, (z + 1) % 2, e - 1, :].bitcast(F32), ALU.subtract).then_inc(sems("pz_ready"), 1)

            early_group(None, 0)
            with eng.Fori(0, EARLY // 2 - 1) as j:
                early_group(0, 1, j)
                early_group(1, 2, j)
            early_group(EARLY - 2, EARLY - 1)
            early_group(EARLY - 1, None)
            E.meet()

        ENGINES = ("pe", "act", "dve")

        def side(eng, me):
            return Side(eng, sems, f"{me}_idle", [f"{o}_idle" for o in ENGINES if o != me])

        @block.sync
        def _(sp):
            sp.dma_start(cst[:], a["consts"]).then_inc(sems("consts_in"), 16)
            sp.dma_start(par[:], a["params"]).then_inc(sems("consts_in"), 16)
            if first:
                sp.dma_start(B["memT"][:], a["memT"].rearrange("(k p) t -> p k t", p=P)).then_inc(sems("mem_in"), 16)
            sp.dma_start(xT[:], a["xT"].rearrange("(k p) t -> p k t", p=P)).then_inc(sems("x_in"), 16)
            for s in range(4):
                sp.dma_start(raw[:, s, :], Wl[0, s]).then_inc(sems(f"raw_in{s}"), 16)
            with sp.Fori(1, n_loop // 4) as j:
                for s in range(4):
                    sp.wait_ge(sems("weights_split"), 4 * j + (s - 3))
                    sp.dma_start(raw[:, s, :], Wl[bass.ds(j, 1), s].rearrange("o p f -> p (o f)")).then_inc(
                        sems(f"raw_in{s}"), 16)
            for t in range(n_loop, N_TILES):
                sp.wait_ge(sems("weights_split"), t - 3)
                sp.dma_start(raw[:, t % 4, :], W[t]).then_inc(sems(f"raw_in{t % 4}"), 16)

        @block.gpsimd
        def _(pool):
            nc.gpsimd.memset(cell[:], 0.0).then_inc(sems("cell_clear"), 1)
            pool.wait_ge(sems("cell_clear"), 1)

            def split_tile(s, t, landed, used, done):
                pool.wait_ge(sems(f"raw_in{s}"), landed)
                if t is None or t >= 2:
                    pool.wait_ge(sems(f"tile_done{s % 2}"), used)
                nc.gpsimd.tensor_tensor(cell[:, 0:1], cell[:, 1:2], cell[:, 1:2], ALU.add)
                nc.gpsimd.tensor_scalar(wH[:, s % 2, :], raw[:, s, :], 1.0, 0.0, ALU.mult, ALU.add).then_inc(
                    sems("weights_hi"), 1)
                pool.wait_ge(sems("weights_hi"), done)
                nc.gpsimd.tensor_tensor(wL[:, s % 2, :], raw[:, s, :], wH[:, s % 2, :].bitcast(F32),
                                        ALU.subtract).then_inc(sems("weights_split"), 1)

            for s in range(4):
                split_tile(s, s, 16, s // 2, s + 1)
            with pool.Fori(1, n_loop // 4) as j:
                for s in range(4):
                    split_tile(s, None, 16 * j + 16, 2 * j + s // 2, 4 * j + (s + 1))
            for t in range(n_loop, N_TILES):
                split_tile(t % 4, t, 16 * (t // 4) + 16, t // 2, t + 1)

        @block.tensor
        def _(pe):
            E = side(pe, "pe")

            def three(out, w, H, L, k, w_slot, start, stop):
                c = slice(P * k, P * k + P)
                pe.matmul(out, wH[:, w_slot, c], H, start=start, stop=False)
                pe.matmul(out, wH[:, w_slot, c], L, start=False, stop=False)
                return pe.matmul(out, wL[:, w_slot, c], H, start=False, stop=stop)

            def one_tile(t, H, L, w=S, j=None, step=0, ready=None):
                def plus(n, per):
                    return n if j is None else n + per * j
                pe.wait_ge(sems("weights_split"), plus(t + 1, step))
                if t >= 2 or j is not None:
                    pe.wait_ge(sems(f"bank_free{t % 2}"), plus(freed(t), step // 2))
                for k in range(8):
                    if ready:
                        ready(k)
                    mm = three(bank(t, w), w, H(k), L(k), k, t % 2, k == 0, k == 7)
                mm.then_inc(sems(f"tile_done{t % 2}"), 1)

            def parts_ready(k):
                if k < KB - 1:
                    E.wait("h_ready")
                else:
                    E.at("rb_used", E.n["made rb"])

            def products(name, n, H, L, w=S, at=0, ready=None):
                t0 = TILE[name] + at
                if n < 4:
                    for t in range(t0, t0 + n):
                        one_tile(t, H, L, w)
                    return
                peeled = 2 if ready or t0 == 0 else 0
                for t in range(peeled):
                    one_tile(t0 + t, H, L, w, ready=None if t else ready)
                t0 += peeled
                with pe.Fori(0, (n - peeled) // 2) as j:
                    for s in range(2):
                        one_tile(t0 + s, H, L, w, j, 2)

            def products_and_sums(name, ready=None):
                for b in range(KB + 2):
                    if b < KB:
                        one_tile(TILE[name] + b, h_hi, h_lo, ready=None if b else ready)
                    if b >= 2:
                        sum_block(E, b == 2)

            def turn(out, in_):
                return nc.tensor.transpose(out, in_, ident)

            h_hi = lambda k: hH[:, k, :]
            h_lo = lambda k: hL[:, k, :]
            pe.wait_ge(sems("consts_in"), 32)

            if first:
                norm_pe(E, **NORMS["mem"])
                m_hi, m_lo = (lambda k: B["mH"][:, k, :]), (lambda k: B["mL"][:, k, :])
                products("ckv", 8, m_hi, m_lo, NMEM, ready=parts_ready)
                for b in range(8):
                    t = TILE["ckv"] + 8 + b
                    one_tile(t, m_hi, m_lo, NMEM)
                    sum_block(E, b == 0)
                    emptied(E, t)
                    E.at("mem_turned", b - 1)
                    for m in range(MB):
                        mm = turn(ps[5 + b % 2][:, m * P:(m + 1) * P], B["vmT"][:, b % 4, m * P:(m + 1) * P])
                    mm.then_inc(sems("mem_turn"), 1)
                norm_pe(E, summed=True, **NORMS["mix"])
                E.arrive()
                products("in_u", 8, h_hi, h_lo, ready=parts_ready)
                products("in_qkv", 8, h_hi, h_lo)

                def exchange(b):
                    emptied(E, TILE["in_qkv"] + b)
                    E.at("roped", b - 1)
                    nc.tensor.matmul(ps[3 + b % 2][:, :], C("swap"), B["qkT"][:, b, :], start=True,
                                     stop=True).then_inc(sems("swapped"), 1)

                for b in range(4):
                    one_tile(TILE["in_qkv"] + 8 + b, h_hi, h_lo,
                             ready=lambda k: exchange(2 * b + k // 5) if k in (4, 7) else None)
                for b in range(4):
                    emptied(E, TILE["in_qkv"] + 8 + b)
                    E.at("v_copied", b - 1)
                    for t in range(TB):
                        mm = turn(ps[5 + b % 2][:, t * P:(t + 1) * P], B["vT"][:, b, t * P:(t + 1) * P])
                    mm.then_inc(sems("v_turned"), 1)
                E.meet()
                units = [(h, i) for h in range(4) for i in range(TB)]

                def scores(u):
                    h, i = units[u]
                    E.at("probs", 2 * (u - 2))
                    for c in range(2):
                        r = slice(64 * c, 64 * c + 64)
                        nc.tensor.matmul(ps[2 * (u % 3) + c][:, 0:P * (i + 1)],
                                                  B["qkT"][r, h, i * P:(i + 1) * P],
                                                  B["qkT"][r, 4 + h, 0:P * (i + 1)], start=True, stop=True).then_inc(sems("scores"), 1)

                scores(0)
                scores(1)
                for u in range(len(units) + 1):
                    if u + 2 < len(units):
                        scores(u + 2)
                    if u < len(units):
                        E.wait("att")
                        E.at("attT", u)
                        for kb in range(units[u][1] + 1):
                            mm = turn(ps[6][:, kb * P:(kb + 1) * P], B["att"][:, u % 2, kb * P:(kb + 1) * P])
                        mm.then_inc(sems("att_turned"), 1)
                    if u >= 1:
                        h, i = units[u - 1]
                        E.at("attT", u)
                        if i == 0:
                            E.at("oT", h)
                        for kb in range(i + 1):
                            mm = nc.tensor.matmul(ps[7][:, i * P:(i + 1) * P], B["vtok"][:, kb, h * P:(h + 1) * P],
                                                  B["attT"][:, (u - 1) % 2, kb * P:(kb + 1) * P], start=(kb == 0), stop=(kb == i))
                        mm.then_inc(sems("pv"), 1)
                E.meet()
                for k in range(4):
                    mm = nc.tensor.matmul(ps[5][:, :], ones, B["cacc"][:, k, :], start=(k == 0), stop=(k == 3))
                mm.then_inc(sems("mean"), 1)
                norm_pe(E, **NORMS["heads"])
                norm_pe(E, **NORMS["ln"])
                E.arrive()
                spread = E.n["made rb"] - 1

                def mixed(k):
                    if k < 4:
                        E.at("rb_used", spread - 3 + k)
                    else:
                        E.wait("conv_parts")

                products_and_sums("out", ready=mixed)
                norm_pe(E, summed=True, **NORMS["cross"])
                E.arrive()
                products("cq", 8, h_hi, h_lo, ready=parts_ready)
                for u in range(17):
                    if u == 0:
                        emptied(E, TILE["cq"] + 6)
                        emptied(E, TILE["cq"] + 7)
                    for n in (0, 1) if u == 0 else (u + 1,) if u < 15 else ():
                        h, i = n // TB, n % TB
                        E.at("probs", 32 + n - 2)
                        for b in range(2):
                            mm = nc.tensor.matmul(ps[(2, 3, 0)[n % 3]][:, 0:NMEM], B["qx"][:, 2 * h + b, i * P:(i + 1) * P],
                                                  B["kmem"][:, 2 * h + b, :], start=(b == 0), stop=(b == 1))
                        mm.then_inc(sems("scores"), 1)
                    if u >= 1:
                        w = u - 1
                        h, i = w // TB, w % TB
                        E.wait("att")
                        E.at("attT", 16 + w - 1)
                        for m in range(MB):
                            mm = turn(ps[4 + w % 2][:, m * P:(m + 1) * P], B["px"][:, w % 2, m * P:(m + 1) * P])
                        mm.then_inc(sems("att_turned"), 1)
                        if i == TB - 1:
                            E.at("attT", 16 + w + 1)
                            E.at("xo_taken", 2 * h)
                            for b in range(2):
                                for m in range(MB):
                                    mm = nc.tensor.matmul(ps[6 + b][:, :], B["vmem"][:, m, (2 * h + b) * P:(2 * h + b + 1) * P],
                                                          B["pxT"][:, h % 2, m, :], start=(m == 0), stop=(m == MB - 1))
                                mm.then_inc(sems("xo"), 1)
                E.meet()
                products_and_sums("co")
                norm_pe(E, summed=True, **NORMS["ffn"])
                E.arrive()
                products("up", 44, h_hi, h_lo, ready=parts_ready)
                E.arrive()
                t0 = TILE["down"]
                for t in range(t0, t0 + 22):
                    pe.wait_ge(sems("weights_split"), t + 1)
                    for k in range(8):
                        d, f = divmod(8 * (t - t0) + k, FFB)
                        if d == 0:
                            E.at("z_parts", f + 1)
                        if f == 0 and d >= 2:
                            E.at("down_taken", d - 1)
                        if f == 4 and d >= 1:
                            sum_block(E, d == 1)
                        mm = three(ps[3 + d % 2][:, :], None, B["zH"][:, f, :], B["zL"][:, f, :], k, t % 2, f == 0, f == FFB - 1)
                        if k == 7:
                            mm.then_inc(sems(f"tile_done{t % 2}"), 1)
                        elif f == FFB - 1:
                            mm.then_inc(sems("down"), 1)
                sum_block(E, False)
                norm_pe(E, summed=True, **NORMS["final"])
            if second:
                second_pe(E, products, products_and_sums, parts_ready, one_tile, turn, h_hi, h_lo)
            else:
                E.meet()

        @block.scalar
        def _(eng):
            E = side(eng, "act")
            eng.wait_ge(sems("consts_in"), 32)

            def copy_tiles(name, n, to, w=S, at=0, func=ACT.Copy):
                for b in range(n):
                    t = TILE[name] + at + b
                    tile_ready(E, t)
                    empties(act.activation(to(b), bank(t, w), func), t)

            def squares_behind(name):
                for b in range(KB):
                    emptied(E, TILE[name] + b)
                    square(E, xT[:, b, :])

            if first:
                E.wait("lam_sums", 2)
                act.activation(sc[:, 2:4], sc[:, 0:2], ACT.Exp).then_inc(sems("lam_exp"), 1)
                eng.wait_ge(sems("mem_in"), 16)
                norm_act(E, **NORMS["mem"])
                copy_tiles("ckv", 8, lambda b: B["kmem"][:, b, :], NMEM)
                eng.wait_ge(sems("x_in"), 16)
                for b in range(8):
                    square(E, xT[:, b, :])
                    if b >= 4:
                        E.at("mem_turn", b - 3)
                    t = TILE["ckv"] + 8 + b
                    tile_ready(E, t)
                    empties(act.activation(B["vmT"][:, b % 4, :], bank(t, NMEM), ACT.Copy), t)
                norm_act(E, squared=True, **NORMS["mix"])
                E.meet()
                eng.dma_start(B["pos"][:], a["pos"].partition_broadcast(P)).then_inc(sems("pos_in"), 16)
                E.wait("angles")
                act.activation(B["sin"][:], B["att"][:, 0, :], ACT.Sin).then_inc(sems("sines"), 1)
                act.activation(B["cos"][:], B["att"][:, 0, :], ACT.Sin, scale=0.5).then_inc(sems("sines"), 1)
                for b in range(4):
                    t = TILE["in_u"] + 2 * b + 1
                    tile_ready(E, t)
                    empties(act.activation(tmp[:, b, :], bank(t), ACT.Sigmoid), t)
                copy_tiles("in_qkv", 8, lambda b: B["qkT"][:, b, :])
                copy_tiles("in_qkv", 4, lambda b: B["vT"][:, b, :], at=8)
                for b in range(4):
                    E.wait("v_turned")
                    act.activation(B["vtok"][:, :, b * P:(b + 1) * P],
                                            ps[5 + b % 2][:, :].rearrange("p (t d) -> p t d", t=TB), ACT.Copy).then_inc(sems("v_copied"), 1)
                E.meet()
                units = [(h, i) for h in range(4) for i in range(TB)]

                def probabilities(u):
                    w = P * (units[u][1] + 1)
                    E.at("att", u - 1)
                    for c in range(2):
                        E.wait("row_max")
                        act.activation(B["p"][:, u % 2, c, 0:w], ps[2 * (u % 3) + c][:, 0:w], ACT.Exp,
                                                bias=ss[:, u % 2, 2 + c:3 + c], scale=0.125,
                                                accum_out=ss[:, u % 2, 4 + c:5 + c]).then_inc(sems("probs"), 1)

                probabilities(0)
                for u, (h, i) in enumerate(units):
                    if u + 1 < len(units):
                        probabilities(u + 1)
                    E.wait("att_turned")
                    E.at("pv", u - 1)
                    act.activation(B["attT"][:, u % 2, 0:P * (i + 1)], ps[6][:, 0:P * (i + 1)], ACT.Copy).then_inc(sems("attT"), 1)
                    if u and i == 0:
                        E.at("pv", u)
                        act.activation(B["oT"][:, h - 1, :], ps[7][:, :], ACT.Copy).then_inc(sems("oT"), 1)
                E.at("pv", len(units))
                act.activation(B["oT"][:, 3, :], ps[7][:, :], ACT.Copy).then_inc(sems("oT"), 1)
                E.meet()
                norm_act(E, **NORMS["heads"])
                E.at("centred", 4)
                norm_act(E, **NORMS["ln"])
                for k in range(4):
                    if k == 0:
                        E.wait("ln_done")
                    act.activation(B["cacc"][:, k, :], B["cacc"][:, k, :], ACT.Silu, bias=PM("ln_b", k)).then_inc(sems("silu"), 1)
                for k in range(4):
                    E.at("silu", k + 1)
                    act.activation(hH[:, 4 + k, :], B["cacc"][:, k, :], ACT.Copy).then_inc(sems("hi_ready"), 1)
                E.meet()
                squares_behind("out")
                norm_act(E, squared=True, **NORMS["cross"])
                E.meet()
                copy_tiles("cq", 8, lambda b: B["qx"][:, b, :])
                for u in range(17):
                    if u < 16:
                        E.wait("row_max")
                        E.at("att_turned", 16 + u - 1)
                        act.activation(B["px"][:, u % 2, :], ps[(2, 3, 0)[u % 3]][:, 0:NMEM], ACT.Exp,
                                                bias=ss[:, u % 2, 2:3], scale=1.0 / 16,
                                                accum_out=ss[:, u % 2, 4:5]).then_inc(sems("probs"), 1)
                    if u >= 1:
                        w = u - 1
                        h, i = w // TB, w % TB
                        E.wait("att_turned")
                        E.at("xo", 2 * (h - 1))
                        act.activation(B["pxT"][:, h % 2, :, i * P:(i + 1) * P],
                                                ps[4 + w % 2][:, 0:NMEM].rearrange("p (m t) -> p m t", m=MB),
                                                ACT.Copy).then_inc(sems("attT"), 1)
                        if i == TB - 1:
                            for b in range(2):
                                E.wait("xo")
                                act.activation(hH[:, 2 * h + b, :], ps[6 + b][:, :], ACT.Copy).then_inc(sems("xo_hi"), 1)
                E.meet()
                squares_behind("co")
                norm_act(E, squared=True, **NORMS["ffn"])
                E.meet()
                for i in range(FFB + 2):
                    if i < FFB:
                        for c in range(2):
                            t = TILE["up"] + 2 * i + c
                            tile_ready(E, t)
                            E.at("ffn_conv", 2 * (i - 2) + c + 1)
                            empties(act.activation(B["uab"][:, i % 2, c, 2:S + 2], bank(t), ACT.Copy), t)
                    if 1 <= i <= FFB:
                        E.at("ffn_conv", 2 * (i - 1) + 2)
                        s = (i - 1) % 2
                        act.activation(sq[:, 2 * s, :], sq[:, 2 * s, :], ACT.Silu).then_inc(sems("ffn_silu"), 1)
                    if i >= 2:
                        hi_part(E, B["zH"][:, i - 2, :])
                E.meet()
                for d in range(8):
                    E.at("down_taken", d + 1)
                    square(E, xT[:, d, :])
                norm_act(E, squared=True, **NORMS["final"])
            if second:
                second_act(E, eng, copy_tiles, squares_behind)
            else:
                E.meet()
            eng.dma_start(a["out"].rearrange("(k p) t -> p k t", p=P), xT[:]).then_inc(sems("out_stored"), 16)
            eng.wait_ge(sems("out_stored"), 16)

        @block.vector
        def _(eng):
            E = side(eng, "dve")
            chain = Chain(eng, sems("dve_step"))
            eng.wait_ge(sems("consts_in"), 32)

            def add_tiles(name, n=8):
                for b in range(n):
                    t = TILE[name] + b
                    tile_ready(E, t)
                    empties(v.tensor_tensor(xT[:, b, :], xT[:, b, :], bank(t), ALU.add), t)

            if first:
                for n in range(2):
                    chain(v.tensor_tensor(tmp[:, n, 0:64], PM("lam", 128 * n, 64), PM("lam", 128 * n + 64, 64), ALU.mult))
                    v.tensor_reduce(sc[:, n:n + 1], tmp[:, n, 0:64], AX, ALU.add).then_inc(sems("lam_sums"), 1)
                chain(v.tensor_scalar(sc[:, 4:5], PM("subln"), 1.0 - 0.2, None, ALU.mult))
                E.wait("lam_exp")
                chain(v.tensor_scalar(sc[:, 6:7], sc[:, 3:4], sc[:, 2:3], -0.2, ALU.subtract, ALU.add))
                eng.wait_ge(sems("mem_in"), 16)
                norm_dve(E, chain, **NORMS["mem"])
                for b in range(8):
                    E.wait("mem_turn")
                    v.tensor_copy(B["vmem"][:, :, b * P:(b + 1) * P],
                                           ps[5 + b % 2][:, 0:NMEM].rearrange("p (m d) -> p m d", m=MB)).then_inc(sems("mem_turned"), 1)
                eng.wait_ge(sems("x_in"), 16)
                norm_dve(E, chain, **NORMS["mix"])
                E.meet()
                ang, y = B["att"][:, 0, :], B["att"][:, 1, :]
                eng.wait_ge(sems("pos_in"), 16)
                chain(v.tensor_copy(B["attT"][:, 0, :], B["pos"][:]))
                chain(v.tensor_scalar(ang, B["attT"][:, 0, :], C("invfreq"), None, ALU.mult))
                magic = 1.5 * 2.0 ** 23
                chain(v.tensor_scalar(y, ang, 1.0 / (2 * math.pi), magic, ALU.mult, ALU.add))
                chain(v.tensor_scalar(y, y, -magic, None, ALU.add))
                c1 = 6.28125
                c2 = float(np.float32(np.floor((2 * math.pi - c1) * 2 ** 21) / 2 ** 21))
                for c in (c1, c2, 2 * math.pi - c1 - c2):
                    chain(v.scalar_tensor_tensor(out=ang, in0=y, scalar=-c, in1=ang, op0=ALU.mult, op1=ALU.add))
                v.tensor_scalar(ang, ang, 3.1415925, -3.1415925, ALU.min, ALU.max).then_inc(sems("angles"), 1)
                E.wait("sines", 2)
                chain(v.tensor_tensor(B["cos"][:], B["cos"][:], B["cos"][:], ALU.mult))
                chain(v.tensor_scalar(B["cos"][:], B["cos"][:], -2.0, 1.0, ALU.mult, ALU.add))
                chain(v.memset(B["cpad"][:, :, 0:TAPS - 1], 0.0))
                for b in range(4):
                    t = TILE["in_u"] + 2 * b
                    tile_ready(E, t)
                    emptied(E, t + 1)
                    empties(v.tensor_tensor(B["cpad"][:, b, TAPS - 1:TAPS - 1 + S], bank(t), tmp[:, b, :], ALU.mult), t)
                units = [(h, i) for h in range(4) for i in range(TB)]

                def taps(a, b):
                    for n in range(a, min(b, 4 * TAPS)):
                        k, m = n // 4, n % 4
                        w = PM("cv_w", m * TAPS + k)
                        x = B["cpad"][:, m, k:k + S]
                        if k == 0:
                            emptied(E, TILE["in_u"] + 2 * m)
                            ins = v.tensor_scalar(B["cacc"][:, m, :], x, w, PM("cv_b", m), ALU.mult, ALU.add)
                        else:
                            E.at("tap", n - 3)
                            ins = v.scalar_tensor_tensor(out=B["cacc"][:, m, :], in0=x, scalar=w,
                                                         in1=B["cacc"][:, m, :], op0=ALU.mult, op1=ALU.add)
                        ins.then_inc(sems("tap"), 1)

                BEFORE, BEHIND = 72, 4 * TAPS - 3 * len(units)
                taps(0, BEFORE)
                for b in range(8):
                    q = B["qkT"][:, b, :]
                    E.wait("swapped")
                    chain(v.tensor_tensor(tmp[:, b % 2, :], ps[3 + b % 2][:, :], B["sin"][:], ALU.mult))
                    chain(v.tensor_tensor(q, q, B["cos"][:], ALU.mult))
                    v.tensor_tensor(q, q, tmp[:, b % 2, :], ALU.add).then_inc(sems("roped"), 1)
                taps(BEFORE, BEHIND)
                E.meet()

                def maxima(u):
                    i = units[u][1]
                    for c in range(2):
                        b = ps[2 * (u % 3) + c]
                        E.wait("scores")
                        chain(v.tensor_tensor(b[:, i * P:(i + 1) * P], b[:, i * P:(i + 1) * P], C("causal"), ALU.add))
                        chain(v.tensor_reduce(ss[:, u % 2, c:c + 1], b[:, 0:P * (i + 1)], AX, ALU.max))
                        v.tensor_scalar(ss[:, u % 2, 2 + c:3 + c], ss[:, u % 2, c:c + 1], -0.125, None, ALU.mult).then_inc(sems("row_max"), 1)

                maxima(0)
                for u, (h, i) in enumerate(units):
                    if u + 1 < len(units):
                        maxima(u + 1)
                    taps(BEHIND + 3 * u, BEHIND + 3 * u + 3)
                    w = P * (i + 1)
                    o = u % 2
                    E.wait("probs", 2)
                    chain(v.reciprocal(ss[:, o, 6:8], ss[:, o, 4:6]))
                    chain(v.tensor_tensor(ss[:, o, 8:9], ss[:, o, 7:8], sc[:, 6:7], ALU.mult))
                    E.at("att_turned", u - 1)
                    chain(v.tensor_scalar(B["att"][:, o, 0:w], B["p"][:, o, 0, 0:w], ss[:, o, 6:7], None, ALU.mult))
                    v.scalar_tensor_tensor(out=B["att"][:, o, 0:w], in0=B["p"][:, o, 1, 0:w], scalar=ss[:, o, 8:9],
                                                    in1=B["att"][:, o, 0:w], op0=ALU.mult, op1=ALU.add).then_inc(sems("att"), 1)
                E.meet()
                E.wait("mean")
                for k in range(4):
                    v.scalar_tensor_tensor(out=B["cacc"][:, k, :], in0=ps[5][:, :], scalar=-1.0 / 512,
                                                    in1=B["cacc"][:, k, :], op0=ALU.mult, op1=ALU.add).then_inc(sems("centred"), 1)
                norm_dve(E, chain, **NORMS["heads"])
                norm_dve(E, chain, **NORMS["ln"])
                E.at("rb_used", 1 + 1 + 4 + 1)
                v.tensor_scalar(sc[:, 9:10], sc[:, 4:5], 1.0, None, ALU.mult).then_inc(sems("ln_done"), 1)
                for k in range(4):
                    E.wait("hi_ready")
                    v.tensor_tensor(hL[:, 4 + k, :], B["cacc"][:, k, :], hH[:, 4 + k, :].bitcast(F32), ALU.subtract).then_inc(sems("conv_parts"), 1)
                E.meet()
                add_tiles("out")
                norm_dve(E, chain, **NORMS["cross"])
                E.meet()
                for u in range(17):
                    if u < 16:
                        E.wait("scores")
                        chain(v.tensor_reduce(ss[:, u % 2, 0:1], ps[(2, 3, 0)[u % 3]][:, 0:NMEM], AX, ALU.max))
                        v.tensor_scalar(ss[:, u % 2, 2:3], ss[:, u % 2, 0:1], -1.0 / 16, None, ALU.mult).then_inc(sems("row_max"), 1)
                    if u >= 1:
                        o = (u - 1) % 2
                        E.wait("probs")
                        chain(v.reciprocal(ss[:, o, 6:7], ss[:, o, 4:5]))
                        v.tensor_scalar(B["px"][:, o, :], B["px"][:, o, :], ss[:, o, 6:7], None, ALU.mult).then_inc(sems("att"), 1)
                        if u % TB == 0:
                            h = (u - 1) // TB
                            for b in range(2):
                                E.wait("xo_hi")
                                v.tensor_tensor(hL[:, 2 * h + b, :], ps[6 + b][:, :], hH[:, 2 * h + b, :].bitcast(F32),
                                                         ALU.subtract).then_inc(sems("xo_taken"), 1)
                E.meet()
                add_tiles("co")
                norm_dve(E, chain, **NORMS["ffn"])
                chain(v.memset(B["uab"][:, :, :, 0:2], 0.0))
                E.meet()
                held = []
                for i in range(FFB + 2):
                    if i < FFB:
                        E.at("v_ready", E.n["made v"])
                        for c in range(2):
                            t = TILE["up"] + 2 * i + c
                            emptied(E, t)
                            u = B["uab"][:, i % 2, c, :]
                            to = sq[:, 2 * (i % 2) + c, :]
                            wcol = 3 * (i + c * FFB)
                            chain(v.tensor_scalar(to, u[:, 2:S + 2], PM("ffn_w", wcol + 2), None, ALU.mult))
                            for k in (1, 0):
                                ins = v.scalar_tensor_tensor(out=to, in0=u[:, k:S + k], scalar=PM("ffn_w", wcol + k), in1=to,
                                                             op0=ALU.mult, op1=ALU.add)
                                if k:
                                    chain(ins)
                            ins.then_inc(sems("ffn_conv"), 1)
                    if 1 <= i <= FFB:
                        E.wait("ffn_silu")
                        s = (i - 1) % 2
                        n = E.made("v")
                        E.at("ffn_conv", 2 * i)
                        v.tensor_tensor(tmp[:, n % 4, :], sq[:, 2 * s, :], sq[:, 2 * s + 1, :], ALU.mult).then_inc(sems("v_ready"), 1)
                        held.append((n, (B["zH"][:, i - 1, :], B["zL"][:, i - 1, :])))
                    if i >= 2:
                        lo_part(E, held.pop(0), name="z_parts")
                E.meet()
                for d in range(8):
                    if d % 4 == 3:
                        tile_ready(E, TILE["down"] + (22 * (d + 1)) // 8 - 1)
                    else:
                        E.wait("down")
                    v.tensor_tensor(xT[:, d, :], xT[:, d, :], ps[3 + d % 2][:, :], ALU.add).then_inc(sems("down_taken"), 1)
                norm_dve(E, chain, **NORMS["final"])
                E.at("rb_used", 1 + 1 + 4 + 1 + 1 + 1 + 1)
                if not second:
                    E.meet()
            if second:
                second_dve(E, eng, chain, add_tiles)


def pack(w):
    k, m = w.shape
    return w.reshape(k // P, P, m // P, P).transpose(2, 1, 0, 3).reshape(m // P, P, k)


def columns(v, n):
    return np.asarray(v).reshape(n, P).T


def first_weights(i):
    w_in, ckv, up, down = i["w_in"][0], i["w_ckv"][0], i["w_up"][0], i["w_down"][0]
    u = pack(w_in[:, 1536:])
    ups = pack(up)
    pairs = lambda t, n: np.stack([t[:n], t[n:]], 1).reshape(2 * n, P, D)
    downs = down.reshape(FFB, P, 8, P).transpose(2, 0, 1, 3).reshape(22, 8, P, P).transpose(0, 2, 1, 3).reshape(22, P, D)
    return [pack(ckv), pairs(u, 4), pack(w_in[:, :1536]), pack(i["w_out"][0]), pack(i["w_cq"][0]),
            pack(i["w_co"][0]), pairs(ups, FFB), downs]


def parameters(i):
    one = lambda v, n: columns(v, n)
    taps = lambda w, n: np.asarray(w).reshape(w.shape[0], n, P).transpose(2, 1, 0).reshape(P, -1)
    rows = lambda v: np.broadcast_to(np.asarray(v).reshape(1, -1), (P, np.asarray(v).size))
    got = [one(i["norm_mix_g"], 8), one(i["norm_cross_g"], 8), one(i["norm_mem_g"], 8), one(i["norm_ffn_g"], 8),
           one(i["norm_final_g"], 8), one(i["mix_norm_w_2"], 8), one(i["ffn_norm_w_2"], 8), one(i["subln_g"], 1),
           taps(i["cv_dw_w"][0], 4), one(i["cv_dw_b"], 4), one(i["cv_ln_g"], 4), one(i["cv_ln_b"], 4),
           taps(i["ffn_dw_w"][0], 44), one(i["sb_q_norm_w_2"], 1), one(i["sb_k_norm_w_2"], 1),
           taps(i["gdn_conv_w_2"][0], 24), one(i["gdn_out_norm_w_2"], 1),
           rows(i["lam_q1"]), rows(i["lam_k1"]), rows(i["lam_q2"]), rows(i["lam_k2"]),
           rows(i["gdn_a_log_2"]), rows(i["gdn_dt_bias_2"])]
    return np.concatenate(got, 1)


def second_weights(i):
    w = i["w_in_2"][0]
    ba = np.concatenate([w[:, 7168:7184], np.zeros((D, P - 16), w.dtype)], 1)
    u = i["peer_u_2"][0].reshape(GROUPS, 8, P, KB, P).transpose(0, 1, 4, 3, 2).reshape(GROUPS, 8, P, D)
    d = i["peer_v_2"][0].reshape(GROUPS, 8, P, KB, P).transpose(0, 3, 2, 1, 4).reshape(GROUPS, 8, P, D)
    peer = [u[:EARLY].reshape(-1, P, D), np.concatenate([u, d], 1)[EARLY:].reshape(-1, P, D), d[:EARLY].reshape(-1, P, D)]
    return [pack(w[:, :3072]), pack(w[:, 7184:8208]), pack(i["w_branch_sb_2"][0]), pack(ba), pack(w[:, 3072:6144]),
            pack(w[:, 6144:7168]), pack(w[:, 8208:9232]), pack(i["w_branch_gdn_2"][0]), pack(i["w_out_2"][0]),
            pack(i["peer_w_q_2"][0])] + peer


def laid_out(i):
    keys = np.stack([i["peer_keys1_2"][0], i["peer_keys2_2"][0]], 1)
    return {
        "weights": np.concatenate(first_weights(i) + second_weights(i)),
        "consts": constants(),
        "params": np.ascontiguousarray(parameters(i)),
        "xT": np.ascontiguousarray(i["x"][0].T),
        "memT": np.ascontiguousarray(i["mem"][0].T),
        "pos": np.ascontiguousarray(i["positions"][0]),
        "keys": np.ascontiguousarray(keys.transpose(0, 1, 3, 2).reshape(2 * NH2, P, P)),
    }


def kernel(**inputs):
    import concourse.bacc as bacc
    from concourse.bass_utils import run_bass_kernel_spmd

    arrays = laid_out({k: np.asarray(v) for k, v in inputs.items()})
    nc = bacc.Bacc("TRN2", target_bir_lowering=False, num_devices=1)
    a = {k: nc.dram_tensor(f"in_{k}", v.shape, mybir.dt.from_np(v.dtype), kind="ExternalInput").ap()
         for k, v in arrays.items()}
    a["out"] = nc.dram_tensor("out_xT", (D, S), F32, kind="ExternalOutput").ap()
    a["gates"] = nc.dram_tensor("gates", (TG, P, P, 32), F32, kind="Internal").ap()
    a["acts"] = nc.dram_tensor("acts", (8 * EARLY, P, S), F32, kind="Internal").ap()
    build(nc, a)
    r = run_bass_kernel_spmd(nc, [{f"in_{k}": v for k, v in arrays.items()}], core_ids=[0])
    return np.ascontiguousarray(r.results[0]["out_xT"].T)[None]
```
